# Optimizing a Trainium2 kernel written in Bass

```python
import math
import jax, jax.numpy as jnp
from jax import lax
import numpy as np

D_MODEL = 1024
BATCH = 1
SEQ = 512
DEPTH = 2

CHUNK = 64
Q_BLOCK = 128
HEAD_DIM = 64
ROPE_THETA = 10000.0
RMS_EPS = 1e-6
SB_HEADS = D_MODEL // 256
SB_WIDTH = SB_HEADS * HEAD_DIM
DIFF_HEADS = D_MODEL // 256
DIFF_VDIM = 2 * HEAD_DIM
DIFF_QK_WIDTH = DIFF_HEADS * 2 * HEAD_DIM
DIFF_WIDTH = DIFF_HEADS * DIFF_VDIM
SWA_HEADS = D_MODEL // 256
SWA_KV_HEADS = max(1, SWA_HEADS // 2)
SWA_WIDTH = SWA_HEADS * HEAD_DIM
SWA_KV_WIDTH = SWA_KV_HEADS * HEAD_DIM
WINDOW = 128
WINDOW_CHUNKS = WINDOW // CHUNK
MIX_WIDTH = SB_WIDTH + DIFF_WIDTH + SWA_WIDTH
IN_WIDTH = 3 * SB_WIDTH + 2 * DIFF_QK_WIDTH + DIFF_WIDTH + SWA_WIDTH + 2 * SWA_KV_WIDTH
D_FF = -(-8 * D_MODEL // (3 * 256)) * 256

kernel_name = "hybrid_stickbreak_diff_swa_sink_block"

def _split_points():
    sizes = (SB_WIDTH, SB_WIDTH, SB_WIDTH, DIFF_QK_WIDTH, DIFF_QK_WIDTH, DIFF_WIDTH,
             SWA_WIDTH, SWA_KV_WIDTH, SWA_KV_WIDTH)
    pts, acc = [], 0
    for s in sizes[:-1]:
        acc += s
        pts.append(acc)
    return pts

def rms_norm(x, g):
    xf = x.astype(jnp.float32)
    y = xf * lax.rsqrt(jnp.mean(xf * xf, axis=-1, keepdims=True) + RMS_EPS)
    return (y * g.astype(jnp.float32)).astype(x.dtype)

def rope_tables(positions):
    inv = 1.0 / (ROPE_THETA ** (jnp.arange(0, HEAD_DIM, 2, dtype=jnp.float32) / HEAD_DIM))
    ang = positions.astype(jnp.float32)[..., None] * inv
    return jnp.cos(ang)[:, :, None, :], jnp.sin(ang)[:, :, None, :]

def apply_rope(x, cos, sin):
    x1, x2 = jnp.split(x.astype(jnp.float32), 2, axis=-1)
    out = jnp.concatenate([x1 * cos - x2 * sin, x2 * cos + x1 * sin], axis=-1)
    return out.astype(x.dtype)

def stick_breaking_attention(q, k, v):
    bsz, s_len, h, d = q.shape
    nb = s_len // Q_BLOCK
    scale = d ** -0.5
    qb = q.reshape(bsz, nb, Q_BLOCK, h, d).transpose(1, 0, 3, 2, 4)
    kpos = jnp.arange(s_len)

    def block(args):
        qi, b = args
        qpos = b * Q_BLOCK + jnp.arange(Q_BLOCK)
        z = jnp.einsum('bhqd,bkhd->bhqk', qi, k, preferred_element_type=jnp.float32) * scale
        causal = (kpos[None, :] < qpos[:, None])[None, None]
        log_keep = jnp.where(causal, -jax.nn.softplus(z), 0.0)
        after = lax.cumsum(log_keep, axis=log_keep.ndim - 1, reverse=True) - log_keep
        w = jnp.exp(jnp.where(causal, -jax.nn.softplus(-z) + after, -jnp.inf))
        return jnp.einsum('bhqk,bkhd->bqhd', w.astype(v.dtype), v)

    out = lax.map(block, (qb, jnp.arange(nb)))
    return out.transpose(1, 0, 2, 3, 4).reshape(bsz, s_len, h * d)

def differential_attention(q, k, v, lam, subln_g, lambda_init):
    bsz, s_len, h, _, d = q.shape
    nb = s_len // Q_BLOCK
    scale = d ** -0.5
    qb = q.reshape(bsz, nb, Q_BLOCK, h, 2, d).transpose(1, 0, 3, 4, 2, 5)
    kchunk = jnp.arange(s_len) // CHUNK

    def block(args):
        qi, b = args
        qchunk = (b * Q_BLOCK + jnp.arange(Q_BLOCK)) // CHUNK
        sc = jnp.einsum('bhcqd,bkhcd->bhcqk', qi, k, preferred_element_type=jnp.float32) * scale
        mask = kchunk[None, :] <= qchunk[:, None]
        p = jax.nn.softmax(jnp.where(mask, sc, -jnp.inf), axis=-1)
        attn = p[:, :, 0] - lam * p[:, :, 1]
        return jnp.einsum('bhqk,bkhe->bqhe', attn.astype(v.dtype), v)

    out = lax.map(block, (qb, jnp.arange(nb)))
    out = out.transpose(1, 0, 2, 3, 4).reshape(bsz, s_len, h, 2 * d)
    out = rms_norm(out, subln_g) * (1.0 - lambda_init)
    return out.reshape(bsz, s_len, h * 2 * d)

def sliding_window_sink_attention(q, k, v, sinks):
    bsz, s_len, hq, d = q.shape
    hkv = k.shape[2]
    g = hq // hkv
    nc = s_len // CHUNK
    scale = d ** -0.5
    qc = q.reshape(bsz, nc, CHUNK, hkv, g, d)

    def band(t):
        tc = t.reshape(bsz, nc, CHUNK, hkv, d)
        tp = jnp.pad(tc, ((0, 0), (WINDOW_CHUNKS - 1, 0), (0, 0), (0, 0), (0, 0)))
        return jnp.concatenate([tp[:, i:i + nc] for i in range(WINDOW_CHUNKS)], axis=2)

    kb, vb = band(k), band(v)
    sc = jnp.einsum('bcqhgd,bckhd->bchgqk', qc, kb, preferred_element_type=jnp.float32) * scale
    key_chunk = (jnp.arange(nc)[:, None] - (WINDOW_CHUNKS - 1)
                 + jnp.arange(WINDOW_CHUNKS * CHUNK)[None, :] // CHUNK)
    valid = (key_chunk >= 0)[None, :, None, None, None, :]
    sc = jnp.where(valid, sc, -jnp.inf)
    sink = jnp.broadcast_to(sinks.astype(jnp.float32).reshape(hkv, g)[None, None, :, :, None, None],
                            sc.shape[:-1] + (1,))
    p = jax.nn.softmax(jnp.concatenate([sc, sink], axis=-1), axis=-1)[..., :-1]
    out = jnp.einsum('bchgqk,bckhd->bcqhgd', p.astype(v.dtype), vb)
    return out.reshape(bsz, s_len, hq * d)

def setup_inputs(seed: int = 0) -> dict:
    key = jax.random.key(seed)
    ks = jax.random.split(key, 20)
    f32 = jnp.float32

    def normal(k, shape, scale):
        return jax.random.normal(k, shape, f32) * scale

    x = normal(ks[0], (BATCH, SEQ, D_MODEL), 1.0)
    offsets = jax.random.randint(ks[1], (BATCH, 1), 0, 64, dtype=jnp.int32) * CHUNK
    positions = offsets + jnp.arange(SEQ, dtype=jnp.int32)[None, :]
    return {
        "x": x,
        "positions": positions,
        "attn_norm_g": 1.0 + normal(ks[2], (DEPTH, D_MODEL), 0.02),
        "w_in": normal(ks[3], (DEPTH, D_MODEL, IN_WIDTH), D_MODEL ** -0.5),
        "diff_q_norm_g": 1.0 + normal(ks[4], (DEPTH, HEAD_DIM), 0.02),
        "diff_k_norm_g": 1.0 + normal(ks[5], (DEPTH, HEAD_DIM), 0.02),
        "diff_lambda": normal(ks[6], (DEPTH, 4, HEAD_DIM), 0.1),
        "diff_subln_g": 1.0 + normal(ks[7], (DEPTH, DIFF_VDIM), 0.02),
        "swa_q_norm_g": 1.0 + normal(ks[8], (DEPTH, HEAD_DIM), 0.02),
        "swa_k_norm_g": 1.0 + normal(ks[9], (DEPTH, HEAD_DIM), 0.02),
        "swa_sinks": normal(ks[10], (DEPTH, SWA_HEADS), 0.5),
        "w_o": normal(ks[11], (DEPTH, MIX_WIDTH, D_MODEL), MIX_WIDTH ** -0.5),
        "ffn_norm_g": 1.0 + normal(ks[12], (DEPTH, D_MODEL), 0.02),
        "w_gate": normal(ks[13], (DEPTH, D_MODEL, D_FF), D_MODEL ** -0.5),
        "w_up": normal(ks[14], (DEPTH, D_MODEL, D_FF), D_MODEL ** -0.5),
        "w_down": normal(ks[15], (DEPTH, D_FF, D_MODEL), D_FF ** -0.5),
    }

def reference(x, positions, attn_norm_g, w_in, diff_q_norm_g, diff_k_norm_g, diff_lambda,
              diff_subln_g, swa_q_norm_g, swa_k_norm_g, swa_sinks, w_o, ffn_norm_g,
              w_gate, w_up, w_down):
    bsz, s_len, _ = x.shape
    cos, sin = rope_tables(positions)
    split_pts = _split_points()
    for l in range(DEPTH):
        lambda_init = 0.8 - 0.6 * math.exp(-0.3 * l)
        h = rms_norm(x, attn_norm_g[l])
        proj = jnp.einsum('bsd,de->bse', h, w_in[l])
        sq, sk, sv, dq, dk, dv, wq, wk, wv = jnp.split(proj, split_pts, axis=-1)

        a_out = stick_breaking_attention(sq.reshape(bsz, s_len, SB_HEADS, HEAD_DIM),
                                         sk.reshape(bsz, s_len, SB_HEADS, HEAD_DIM),
                                         sv.reshape(bsz, s_len, SB_HEADS, HEAD_DIM))

        dq = apply_rope(rms_norm(dq.reshape(bsz, s_len, 2 * DIFF_HEADS, HEAD_DIM), diff_q_norm_g[l]), cos, sin)
        dk = apply_rope(rms_norm(dk.reshape(bsz, s_len, 2 * DIFF_HEADS, HEAD_DIM), diff_k_norm_g[l]), cos, sin)
        lam_vecs = diff_lambda[l].astype(jnp.float32)
        lam = (jnp.exp(jnp.sum(lam_vecs[0] * lam_vecs[1]))
               - jnp.exp(jnp.sum(lam_vecs[2] * lam_vecs[3])) + lambda_init)
        b_out = differential_attention(dq.reshape(bsz, s_len, DIFF_HEADS, 2, HEAD_DIM),
                                       dk.reshape(bsz, s_len, DIFF_HEADS, 2, HEAD_DIM),
                                       dv.reshape(bsz, s_len, DIFF_HEADS, DIFF_VDIM),
                                       lam, diff_subln_g[l], lambda_init)

        wq = apply_rope(rms_norm(wq.reshape(bsz, s_len, SWA_HEADS, HEAD_DIM), swa_q_norm_g[l]), cos, sin)
        wk = apply_rope(rms_norm(wk.reshape(bsz, s_len, SWA_KV_HEADS, HEAD_DIM), swa_k_norm_g[l]), cos, sin)
        c_out = sliding_window_sink_attention(wq, wk, wv.reshape(bsz, s_len, SWA_KV_HEADS, HEAD_DIM),
                                              swa_sinks[l])

        mix = jnp.concatenate([a_out, b_out, c_out], axis=-1)
        x = x + jnp.einsum('bse,ed->bsd', mix, w_o[l])

        h = rms_norm(x, ffn_norm_g[l])
        ff = jax.nn.silu(jnp.einsum('bsd,df->bsf', h, w_gate[l])) * jnp.einsum('bsd,df->bsf', h, w_up[l])
        x = x + jnp.einsum('bsf,fd->bsd', ff, w_down[l])
    return x


_drawn_inputs = setup_inputs


def setup_inputs(seed=0):
    import zlib

    import numpy as np

    out = dict(_drawn_inputs(seed))
    spreads = {}
    factors = {'diff_q_norm_g': 4.927,
     'diff_k_norm_g': 4.25,
     'diff_subln_g': 3.945,
     'swa_q_norm_g': 8.0,
     'swa_k_norm_g': 8.0,
     'swa_sinks': 8.0,
     'ffn_norm_g': 3.261}
    for name, (base, spread) in spreads.items():
        noise = np.random.default_rng([zlib.crc32(name.encode()), seed]).standard_normal(out[name].shape)
        drawn = base * np.exp(spread * noise) if base else spread * noise
        out[name] = __import__('jax').numpy.asarray(drawn.astype(out[name].dtype))
    for name, factor in factors.items():
        out[name] = (out[name] * factor).astype(out[name].dtype)
    return out
```

```python
from contextlib import ExitStack

import concourse.bass as bass
import numpy as np
from concourse import mybir

F32 = mybir.dt.float32
F32R = mybir.dt.float32r
BF16 = mybir.dt.bfloat16
I32 = mybir.dt.int32
ACT = mybir.ActivationFunctionType
ALU = mybir.AluOpType
AX_X = mybir.AxisListType.X

P = 128
D_MODEL = 1024
SEQ = 512
DEPTH = 2
HD = 64
CHUNK = 64
ROPE_THETA = 10000.0
EPS = 1e-6
D_FF = -(-8 * D_MODEL // (3 * 256)) * 256
SCALE = HD ** -0.5
KT = D_MODEL // P
FT = D_FF // P
NB = SEQ // P
NEG = -1e30

GROUPS = [("sb", 0), ("sb", 1), ("swa", 0), ("diff", 0), ("diff", 1), ("diff", 2), ("diff", 3)]
TILES = []
for _g, (_kind, _i) in enumerate(GROUPS):
    for _role in (["q0", "q1", "k", "v"] if _kind == "swa" else ["q0", "k", "v"]):
        TILES.append((_g, _role))
NT = len(TILES)
MIX_OF = {0: [0], 1: [1], 2: [2, 3], 3: [4], 4: [5], 5: [6], 6: [7]}
QSLOT = {(0, "q0"): 0, (1, "q0"): 1, (2, "q0"): 0, (2, "q1"): 2, (3, "q0"): 1, (4, "q0"): 0, (5, "q0"): 1, (6, "q0"): 0}

HALF = FT // 2
N8 = NT + KT + 2 * FT
N11 = 2 * KT
WPER = N8 + N11
RING = 3
assert WPER % RING == 0 and (NT + KT) % RING == 0
A_WO, A_GU, A_DOWN = NT, NT + KT, NT + KT + 2 * FT
ACCS = A_DOWN + KT

C_FG, C_NG, C_DQ, C_DK, C_WQ, C_WK, C_SUB, C_SINK, C_NLAM, NPAR = 0, 8, 16, 17, 18, 19, 20, 21, 25, 26
K_ID, K_BLK, K_ONE, K_TRI, K_NEG1, K_MSB, K_MSW, K_MDF, NCONST = (P * i for i in range(9))


class Signal:

    def __init__(self, sem, events, before=0):
        self.sem, self.before = sem, before
        self.count = {e: i + 1 for i, e in enumerate(events)}
        self.per = len(events)

    def after(self, L, event):
        return L * self.per + (self.before + self.count[event])

    def nth(self, L, n):
        return L * self.per + (n + self.before)


def attention_pieces(g):
    kind = GROUPS[g][0]
    if kind == "sb":
        return [("z", g, 0), ("cum", g, 0), ("z", g, 1), ("pv", g, 0), ("cum", g, 1), ("pv", g, 1), ("mix", g, 0)]
    if kind == "diff":
        return [("s", g, 0), ("s", g, 1), ("x", g, 0), ("s", g, 2), ("x", g, 1), ("s", g, 3), ("x", g, 2),
                ("x", g, 3), ("pv", g, 0), ("mix", g, 0), ("mixn", g, 0)]
    out = []
    for hd in range(4):
        out += [("s", g, (hd, 0)), ("s", g, (hd, 1))]
        out += [("x", g, (hd, 0)), ("x", g, (hd, 1)), ("pv", g, hd)]
        if hd % 2:
            out.append(("mix", g, hd // 2))
    return out


def attention_steps():
    steps, queue = [], []
    for t, (g, role) in enumerate(TILES):
        steps.append(("proj", t))
        if t == 0:
            steps.append(("rstd", 0))
            continue
        if TILES[t - 1][1] == "v":
            steps += queue
            steps.append(("post", t - 1))
            queue = attention_pieces(TILES[t - 1][0])
            n = 1
        else:
            steps.append(("post", t - 1))
            n = -(-len(queue) // 2) if role == "k" else -(-len(queue) // 2)
        steps += queue[:n]
        queue = queue[n:]
    steps += queue
    steps.append(("post", NT - 1))
    steps += attention_pieces(TILES[-1][0])
    return steps


STEPS = attention_steps()


def roped(t):
    return GROUPS[TILES[t][0]][0] != "sb" and TILES[t][1] != "v"


def units_of(step):
    _, g, b = step
    return [(g, b, 0), (g, b, 1)] if GROUPS[g][0] == "diff" else [(g, b, 0)]


UNITS = [u for s in STEPS if s[0] == "s" for u in units_of(s)]
T_USES = [s for s in STEPS if s[0] in ("rstd", "x", "mixn") or (s[0] == "post" and (roped(s[1]) or TILES[s[1]][1] == "v"))]
T_USES.append(("rstd", 1))
T_BOTH = [s for s in T_USES if s[0] == "x" or (s[0] == "post" and TILES[s[1]][1] == "v")]


def trunk_kernel(nc, x_in, pos_in, w8_in, w11_in, par_in, lam_in, misc_in, const_in, out):
    ctx = ExitStack()
    with ctx:
        def sb(name, cols, dt=F32):
            return ctx.enter_context(nc.sbuf_tensor(name, [P, cols], dt))

        def sem(name):
            return ctx.enter_context(nc.semaphore(name))

        X = sb("X", KT * SEQ)
        H = sb("H", 2 * KT * SEQ, F32R)
        raw = sb("raw", RING * HALF * P)
        W = sb("W", RING * 2 * HALF * P, F32R)
        R = sb("R", 2 * FT * SEQ, F32R)
        tables = sb("tables", 2 * SEQ)
        pbuf = sb("pbuf", 2 * SEQ)
        work = sb("work", 4 * SEQ)
        MRN = sb("MRN", SEQ)
        U = sb("U", 6 * SEQ)
        rstd = sb("rstd", SEQ)
        par = sb("par", DEPTH * NPAR)
        gain0 = sb("gain0", KT)
        cur = sb("cur", NPAR)
        lam = MRN[:, 0:DEPTH * 4 * HD]
        lamw = sb("lamw", 8 * DEPTH)
        misc = sb("misc", 8)
        const = sb("const", 3 * P)
        constr = sb("constr", 2 * P, F32R)
        constb = sb("constb", 4 * P, BF16)
        stat = sb("stat", 32)
        idle = sb("idle", 2)

        def rpart(at, n):
            return R[:, at * SEQ:(at + n) * SEQ]
        mix = [rpart(0, KT), rpart(KT, KT)]
        qbuf = [[rpart(16 + 2 * s, 1), rpart(17 + 2 * s, 1)] for s in range(2)] + [[rpart(41, 1), rpart(42, 1)]]
        kbuf = [[rpart(20 + 2 * s, 1), rpart(21 + 2 * s, 1)] for s in range(2)]
        vbuf = [rpart(24 + 2 * s, 2).rearrange("p (j a e) -> p j a e", j=NB, a=2) for s in range(2)]
        pt = [rpart(28 + 4 * s, 4).rearrange("p (j q) -> p j q", j=NB) for s in range(2)]
        spb = [R[:, 36 * SEQ:36 * SEQ + 1280], R[:, 36 * SEQ + 1280:36 * SEQ + 2560]]
        ff = [rpart(0, FT), rpart(FT, FT)]
        SQ, RN, Y, ROT = (work[:, i * SEQ:(i + 1) * SEQ] for i in range(4))
        MSQ = U[:, 4 * SEQ:5 * SEQ]
        ssum = ROT
        COS, SIN = tables[:, 0:SEQ], tables[:, SEQ:2 * SEQ]
        E = U[:, 0:1280]
        eb = [U[:, i * SEQ:(i + 1) * SEQ] for i in range(4)]
        at = [U[:, (4 + i) * SEQ:(5 + i) * SEQ] for i in range(2)]
        gbuf = [U[:, i * SEQ:(i + 1) * SEQ] for i in range(3)]
        ubuf = [U[:, (3 + i) * SEQ:(4 + i) * SEQ] for i in range(3)]
        ident, blk, ones = (const[:, i * P:(i + 1) * P] for i in range(3))
        tri, neg1 = constr[:, 0:P], constr[:, P:2 * P]
        identb, msb = constb[:, 0:P], constb[:, P:2 * P]
        msw, mdf = constb[:, 2 * P:4 * P], constb[:, 3 * P:4 * P]
        eps, one = misc[:, 2:3], misc[:, 3:4]

        banks = [ctx.enter_context(nc.psum_tensor(f"bank{i}", [P, 512], F32)) for i in range(8)]
        acc = banks[0:2]
        Z = banks[2:5]
        O = banks[5]
        T = banks[6:8]
        gubank = banks[0:6]
        downbank = banks[2:5]
        zreg = [(0, 0, 512), (1, 0, 384), (2, 0, 256), (1, 384, 128)]
        eoff = [0, 512, 1024, 896]

        def zpart(j, skip=0):
            b, c, n = zreg[j]
            return Z[b][:, c + skip:c + n]

        def epart(buf, j):
            return buf[:, eoff[j]:eoff[j] + SEQ - P * j]
        ZE = [(0, 0, 512), (1, 512, 512), (2, 1024, 256)]

        loaded, xin = sem("loaded"), sem("x_loaded")
        prep = sem("prepared")
        raw_ready = [sem(f"raw_ready{s}") for s in range(RING)]
        w_hi = sem("w_hi_done")
        out_done = sem("out_done")
        tiles8 = [("wo", d) for d in range(KT)] + [("down", d) for d in range(KT)]
        proj = [("proj", t) for t in range(NT)]
        acc_names = proj + [("wo", d) for d in range(KT)] + [(r, f) for f in range(FT) for r in "gu"] + [("down", d) for d in range(KT)]
        w_ready = Signal(sem("w_ready"), range(WPER), before=RING)
        blocks_done = Signal(sem("blocks_done"), range(WPER), before=RING)
        acc_free = Signal(sem("acc_free"), acc_names)
        t_ready = Signal(sem("t_ready"), T_USES)
        t_act = Signal(sem("t_read_act"), T_USES)
        t_dve = Signal(sem("t_read_dve"), T_BOTH)
        zs = [s for s in STEPS if s[0] in ("z", "cum")]
        z_names = [n for s in STEPS for n in (units_of(s) if s[0] == "s" else [s] if s[0] in ("z", "cum") else [])]
        z_ready = Signal(sem("z_ready"), z_names)
        pvs = [s for s in STEPS if s[0] == "pv"]
        pv_done = Signal(sem("pv_done"), pvs)
        heads = [s for s in STEPS if s[0] == "z"]
        e_ready = Signal(sem("ln_ready"), heads)
        sp_ready = Signal(sem("softplus_ready"), heads)
        w_exp = Signal(sem("weights_exp"), heads)
        w_split = Signal(sem("weights_split"), heads)
        negmax = Signal(sem("negmax_ready"), UNITS)
        exps = Signal(sem("exp_ready"), UNITS)
        ss = [s for s in STEPS if s[0] == "s"]
        at_ready = Signal(sem("probs_ready"), ss)
        rope_t = [t for t in range(NT) if roped(t)]
        sbqk = [t for t in range(NT) if not roped(t) and TILES[t][1] != "v"]
        sq_ready = Signal(sem("squares_ready"), rope_t)
        rn_ready = Signal(sem("headnorm_ready"), rope_t)
        qk_hi = Signal(sem("qk_hi_ready"), sbqk)
        qk_ready = Signal(sem("qk_ready"), [t for t in range(NT) if TILES[t][1] != "v"])
        mixes = [s for s in STEPS if s[0] == "mix"]
        mixns = [s for s in STEPS if s[0] == "mixn"]
        mix_act = Signal(sem("mix_act"), mixes)
        mrn_ready = Signal(sem("mixnorm_ready"), mixns)
        mix_ready = Signal(sem("mix_ready"), range(KT))
        h_hi = Signal(sem("h_hi_ready"), tiles8, before=KT)
        x_sq = Signal(sem("x_squares"), tiles8, before=KT)
        h_ready = Signal(sem("h_ready"), tiles8, before=KT)
        ssum_ready = Signal(sem("ssum_ready"), ["wo", "down"], before=1)
        rstd_ready = Signal(sem("rstd_ready"), [0, 1])
        silu = Signal(sem("silu_ready"), range(FT))
        zeroed = Signal(sem("values_zeroed"), [0])
        ffr = Signal(sem("ff_ready"), range(FT))

        block = ctx.enter_context(nc.Block())

        def mix_tile(step):
            _, g, i = step
            return MIX_OF[g][i]

        def last_pv(step):
            return [s for s in pvs if STEPS.index(s) < STEPS.index(("mix",) + step[1:])][-1]

        def previous(names, name):
            i = names.index(name)
            return names[i - 1] if i else None

        def pt_parts(step):
            _, g, b = step
            if GROUPS[g][0] == "diff":
                return [(slice(0, b + 1), b, 0, b + 1)]
            out_ = []
            for i in range(2):
                bb = 2 * b[1] + i
                j0 = max(bb - 1, 0)
                out_.append((slice(j0, bb + 1), bb, 2 * i + (1 if bb == 0 else 0), 2 * i + 2))
            return out_

        @block.sync
        def _(sp):
            for k in range(KT):
                sp.dma_start(X[:, k * SEQ:(k + 1) * SEQ], x_in[k]).then_inc(xin, 16)
            sp.dma_start(par[:, :], par_in[:, KT:]).then_inc(loaded, 16)
            sp.dma_start(gain0[:, :], par_in[:, 0:KT]).then_inc(loaded, 16)
            sp.dma_start(misc[:, :], misc_in).then_inc(loaded, 16)
            sp.dma_start(const[:, :], const_in[:, 0:3 * P]).then_inc(loaded, 16)
            sp.dma_start(U[:, 0:NCONST - 3 * P], const_in[:, 3 * P:NCONST]).then_inc(loaded, 16)
            sp.dma_start(lam, lam_in).then_inc(loaded, 16)
            sp.dma_start(pbuf[:, 0:SEQ].bitcast(I32), pos_in).then_inc(loaded, 16)

            def load(L, n, src, cols, slot):
                sp.wait_ge(w_ready.sem, L * WPER + (n + 1))
                sp.dma_start(raw[:, slot * HALF * P:slot * HALF * P + cols], src).then_inc(raw_ready[slot], 16)

            with sp.Fori(0, DEPTH) as L:
                with sp.Fori(0, N8 // RING) as i:
                    for s in range(RING):
                        load(L, i * RING + s, w8_in[bass.ds(L * N8 + i * RING + s, 1)].rearrange("o p c -> p (o c)"), KT * P, s)
                for n in range(N8 // RING * RING, N8):
                    load(L, n, w8_in[bass.ds(L * N8 + n, 1)].rearrange("o p c -> p (o c)"), KT * P, n % RING)
                load(L, N8, w11_in[bass.ds(L * N11, 1)].rearrange("o p c -> p (o c)"), HALF * P, N8 % RING)
                with sp.Fori(0, (N11 - 1) // RING) as i:
                    for s in range(RING):
                        n = i * RING + s + 1
                        load(L, n + N8, w11_in[bass.ds(L * N11 + n, 1)].rearrange("o p c -> p (o c)"), HALF * P, (N8 + 1 + s) % RING)
            for d in range(KT):
                sp.wait_ge(acc_free.sem, acc_free.after(DEPTH - 1, ("down", d)))
                sp.dma_start(out[d], X[:, d * SEQ:(d + 1) * SEQ]).then_inc(out_done, 16)
            sp.wait_ge(out_done, 16 * KT)

        @block.gpsimd
        def _(pool):
            nc.gpsimd.memset(idle[:, 0:1], 0.0).then_inc(w_ready.sem, RING)
            pool.wait_ge(w_ready.sem, RING)

            def split(L, n, turn, cols, slot):
                src = raw[:, slot * HALF * P:slot * HALF * P + cols]
                hi = W[:, 2 * slot * HALF * P:2 * slot * HALF * P + cols]
                lo = W[:, (2 * slot + 1) * HALF * P:(2 * slot + 1) * HALF * P + cols]
                pool.wait_ge(blocks_done.sem, L * WPER + (n + 1))
                pool.wait_ge(raw_ready[slot], L * (16 * WPER // RING) + (turn + 1) * 16)
                nc.gpsimd.tensor_tensor(idle[:, 1:2], idle[:, 0:1], idle[:, 0:1], ALU.mult)
                nc.gpsimd.tensor_copy(hi, src).then_inc(w_hi, 1)
                pool.wait_ge(w_hi, L * WPER + (n + 1))
                nc.gpsimd.tensor_tensor(lo, src, hi.bitcast(F32), ALU.subtract).then_inc(w_ready.sem, 1)

            with pool.Fori(0, DEPTH) as L:
                with pool.Fori(0, N8 // RING) as i:
                    for s in range(RING):
                        split(L, i * RING + s, i, KT * P, s)
                for n in range(N8 // RING * RING, N8):
                    split(L, n, n // RING, KT * P, n % RING)
                split(L, N8, N8 // RING, HALF * P, N8 % RING)
                with pool.Fori(0, (N11 - 1) // RING) as i:
                    for s in range(RING):
                        n0 = N8 + 1 + s
                        split(L, i * RING + n0, i + n0 // RING, HALF * P, n0 % RING)

        @block.tensor
        def _(pe):
            def whalf(slot, part, k):
                at0 = (2 * slot + part) * HALF * P + k * P
                return W[:, at0:at0 + P]

            def three(out_, a, b, first, last, **kw):
                nc.tensor.matmul(out_, a[0], b[0], start=first, stop=False, **kw)
                nc.tensor.matmul(out_, a[0], b[1], start=False, stop=False, **kw)
                return nc.tensor.matmul(out_, a[1], b[0], start=False, stop=last, **kw)

            def wblock(L, n, slot, out_, rhs, ks, first, last):
                pe.wait_ge(w_ready.sem, w_ready.nth(L, n + 1))
                for i, k in enumerate(ks):
                    mm = three(out_, (whalf(slot, 0, i), whalf(slot, 1, i)),
                               (rhs[0][:, k * SEQ:(k + 1) * SEQ], rhs[1][:, k * SEQ:(k + 1) * SEQ]),
                               first and i == 0, last and i == len(ks) - 1)
                return mm

            Hs = [H[:, 0:KT * SEQ], H[:, KT * SEQ:2 * KT * SEQ]]

            def t_bank(L, use):
                u = T_USES.index(use)
                if u >= 2:
                    old = T_USES[u - 2]
                    pe.wait_ge(t_act.sem, t_act.after(L, old))
                    if old in T_BOTH:
                        pe.wait_ge(t_dve.sem, t_dve.after(L, old))
                return T[u % 2]

            z_owner = {}

            def take_z(L, bank, step):
                if bank in z_owner:
                    old = z_owner[bank]
                    s = w_exp if old[0] == "z" else exps
                    pe.wait_ge(s.sem, s.after(L, old))
                z_owner[bank] = step

            def rstd_sum(L, n):
                bank = t_bank(L, ("rstd", n))
                pe.wait_ge(ssum_ready.sem, L * 2 + (n + 1))
                nc.tensor.matmul(bank[:, :], ones, ssum, start=True, stop=True).then_inc(t_ready.sem, 1)

            def step_proj(L, t):
                if t >= 2:
                    pe.wait_ge(acc_free.sem, acc_free.after(L, ("proj", t - 2)))
                pe.wait_ge(w_ready.sem, w_ready.nth(L, t + 1))
                for k in range(KT):
                    if t == 0:
                        pe.wait_ge(h_ready.sem, L * 16 + (k + 1))
                    mm = three(acc[t % 2][:, :], (whalf(t % RING, 0, k), whalf(t % RING, 1, k)),
                               (Hs[0][:, k * SEQ:(k + 1) * SEQ], Hs[1][:, k * SEQ:(k + 1) * SEQ]), k == 0, k == KT - 1)
                mm.then_inc(blocks_done.sem, 1)

            def step_post(L, t):
                g, role = TILES[t]
                use = ("post", t)
                if roped(t):
                    bank = t_bank(L, use)
                    pe.wait_ge(sq_ready.sem, sq_ready.after(L, t))
                    nc.tensor.matmul(bank[:, :], blk, SQ, start=True, stop=True).then_inc(t_ready.sem, 1)
                elif role == "v":
                    bank = t_bank(L, use)
                    pe.wait_ge(acc_free.sem, acc_free.after(L, ("proj", t)))
                    for j in range(NB):
                        mm = nc.tensor.transpose(bank[:, j * P:(j + 1) * P], pbuf[:, (t % 2) * SEQ + j * P:(t % 2) * SEQ + (j + 1) * P], ident)
                    mm.then_inc(t_ready.sem, 1)

            def tile_of(g, role):
                return TILES.index((g, role))

            def step_z(L, g, h):
                pe.wait_ge(qk_ready.sem, qk_ready.after(L, tile_of(g, "k")))
                for b in range(3):
                    take_z(L, b, ("z", g, h))
                r = slice(HD * h, HD * h + HD)
                q, k = qbuf[QSLOT[g, "q0"]], kbuf[g % 2]
                for j in range(NB):
                    keys, qs = slice(P * j, P * j + P), slice(P * j, SEQ)
                    nc.tensor.matmul(zpart(j), k[0][r, keys], q[0][r, qs], start=j < 3, stop=False, skip_group_check=True)
                    nc.tensor.matmul(zpart(j)[:, 0:P], identb, msb, start=False, stop=False, skip_group_check=True)
                    nc.tensor.matmul(zpart(j), k[0][r, keys], q[1][r, qs], start=False, stop=False, skip_group_check=True)
                    mm = nc.tensor.matmul(zpart(j), k[1][r, keys], q[0][r, qs], start=False, stop=True, skip_group_check=True)
                mm.then_inc(z_ready.sem, 1)

            def step_cum(L, g, h):
                pe.wait_ge(sp_ready.sem, sp_ready.after(L, ("z", g, h)))
                for j in range(NB):
                    for i in range(NB - 1, j - 1, -1):
                        for part in range(2):
                            mm = nc.tensor.matmul(zpart(j, P * (i - j)), tri if i == j else neg1, epart(spb[part], i),
                                                  start=False, stop=(i == j and part == 1), skip_group_check=True)
                mm.then_inc(z_ready.sem, 1)

            def first_pv(step):
                before = [s for s in STEPS[:STEPS.index(step)] if s[0] in ("mix", "pv")]
                return not before or before[-1][0] == "mix"

            def step_pv(L, step):
                _, g, h = step
                kind = GROUPS[g][0]
                start = first_pv(step)
                if start:
                    m = min(mix_tile(s) for s in mixes if STEPS.index(s) > STEPS.index(step))
                    if m:
                        pe.wait_ge(mix_ready.sem, mix_ready.after(L, m - 1))
                if kind == "sb":
                    pe.wait_ge(w_split.sem, w_split.after(L, ("z", g, h)))
                    pe.wait_ge(t_dve.sem, t_dve.after(L, ("post", tile_of(g, "v"))))
                else:
                    lastx = ("x", g, NB - 1) if kind == "diff" else ("x", g, (h, 1))
                    pe.wait_ge(t_dve.sem, t_dve.after(L, lastx))
                half = 0 if kind == "diff" else h % 2
                end = kind == "diff" or h % 2 == 1
                for j in range(NB):
                    qs = slice(P * j, min(P * (j + 2), SEQ) if kind == "swa" else SEQ)
                    vv = (vbuf[0][:, j, half, :], vbuf[1][:, j, half, :])
                    pp = (pt[0][:, j, qs], pt[1][:, j, qs])
                    mm = three(O[:, qs], vv, pp, start and j == 0, end and j == NB - 1, skip_group_check=True)
                mm.then_inc(pv_done.sem, 1)

            def step_s(L, step):
                _, g, b = step
                kind = GROUPS[g][0]
                for (u, c) in ((u, u[2]) for u in units_of(step)):
                    bank = UNITS.index(u) % 3
                    take_z(L, bank, u)
                    z = Z[bank]
                    kk = kbuf[g % 2]
                    pe.wait_ge(qk_ready.sem, qk_ready.after(L, tile_of(g, "k")))
                    if kind == "diff":
                        q, r = qbuf[QSLOT[g, "q0"]], slice(HD * c, HD * c + HD)
                        qs, ks, o, m = slice(P * b, P * b + P), slice(0, P * (b + 1)), z[:, 0:P * (b + 1)], z[:, P * b:P * b + P]
                        parts = [(qs, ks, o, m, mdf)]
                    else:
                        hd, bp = b
                        q, r = qbuf[QSLOT[g, f"q{hd // 2}"]], slice(HD * (hd % 2), HD * (hd % 2) + HD)
                        parts = []
                        for i in range(2):
                            bb = 2 * bp + i
                            lo = P if bb == 0 else 0
                            o = z[:, 2 * P * i + lo:2 * P * (i + 1)]
                            parts.append((slice(P * bb, P * bb + P), slice(P * (bb - 1) + lo, P * (bb + 1)), o, o, mdf if bb == 0 else msw))
                    for n, (qs, ks, o, m, mask) in enumerate(parts):
                        nc.tensor.matmul(o, q[0][r, qs], kk[0][r, ks], start=n == 0, stop=False, skip_group_check=True)
                        nc.tensor.matmul(m, identb, mask, start=False, stop=False, skip_group_check=True)
                        nc.tensor.matmul(o, q[0][r, qs], kk[1][r, ks], start=False, stop=False, skip_group_check=True)
                        mm = nc.tensor.matmul(o, q[1][r, qs], kk[0][r, ks], start=False, stop=True, skip_group_check=True)
                    mm.then_inc(z_ready.sem, 1)

            def step_x(L, step):
                _, g, b = step
                bank = t_bank(L, step)
                pe.wait_ge(at_ready.sem, at_ready.after(L, ("s", g, b)))
                src = at[ss.index(("s", g, b)) % 2]
                n0, n1 = (0, b + 1) if GROUPS[g][0] == "diff" else (1 if b[1] == 0 else 0, 4)
                for j in range(n0, n1):
                    mm = nc.tensor.transpose(bank[:, j * P:(j + 1) * P], src[:, j * P:(j + 1) * P], ident)
                mm.then_inc(t_ready.sem, 1)

            def step_mixn(L, step):
                bank = t_bank(L, step)
                pe.wait_ge(mix_act.sem, mix_act.after(L, ("mix",) + step[1:]))
                nc.tensor.matmul(bank[:, :], ones, MSQ, start=True, stop=True).then_inc(t_ready.sem, 1)

            def out_tile(L, d):
                a = acc[d % 2]
                pe.wait_ge(acc_free.sem, acc_free.nth(L, A_WO + d - 1))
                pe.wait_ge(w_ready.sem, w_ready.nth(L, NT + d + 1))
                slot = (NT + d) % RING
                for k in range(KT):
                    if d == 0:
                        pe.wait_ge(mix_ready.sem, mix_ready.after(L, k))
                    mm = three(a[:, :], (whalf(slot, 0, k), whalf(slot, 1, k)),
                               (mix[0][:, k * SEQ:(k + 1) * SEQ], mix[1][:, k * SEQ:(k + 1) * SEQ]), k == 0, k == KT - 1)
                mm.then_inc(blocks_done.sem, 1)

            def gate_up(L, f, r, first=False):
                for i in range(2):
                    n = f * 2 + i
                    bank = gubank[2 * r + i]
                    if not first:
                        pe.wait_ge(acc_free.sem, acc_free.nth(L, n + (A_GU - 5)))
                    elif r == 0:
                        pe.wait_ge(acc_free.sem, acc_free.nth(L, A_GU - 1 + i))
                    if i == 0 and first and r == 0:
                        pe.wait_ge(h_ready.sem, L * 16 + 16)
                    mm = wblock(L, n + A_GU, (2 * r + i) % RING, bank[:, :], Hs, range(KT), True, True)
                    mm.then_inc(blocks_done.sem, 1)

            def down_tile(L, d, r):
                bank = downbank[r]
                pe.wait_ge(acc_free.sem, acc_free.nth(L, d + (A_DOWN - 2)))
                for half in range(2):
                    n = d * 2 + (N8 + half)
                    slot = (N8 + 2 * r + half) % RING
                    pe.wait_ge(w_ready.sem, w_ready.nth(L, n + 1))
                    for i in range(HALF):
                        k = HALF * half + i
                        if k in (0, FT - 1):
                            pe.wait_ge(ffr.sem, ffr.nth(L, FT - 1 if k == 0 else FT))
                        mm = three(bank[:, :], (whalf(slot, 0, i), whalf(slot, 1, i)),
                                   (ff[0][:, k * SEQ:(k + 1) * SEQ], ff[1][:, k * SEQ:(k + 1) * SEQ]), k == 0, k == FT - 1)
                    mm.then_inc(blocks_done.sem, 1)

            pe.wait_ge(prep, 1)
            nc.tensor.sem_inc(blocks_done.sem, RING)
            with pe.Fori(0, DEPTH) as L:
                z_owner.clear()
                for s in STEPS:
                    if s[0] == "proj":
                        step_proj(L, s[1])
                    elif s[0] == "rstd":
                        rstd_sum(L, 0)
                    elif s[0] == "post":
                        step_post(L, s[1])
                    elif s[0] == "z":
                        step_z(L, s[1], s[2])
                    elif s[0] == "cum":
                        step_cum(L, s[1], s[2])
                    elif s[0] == "pv":
                        step_pv(L, s)
                    elif s[0] == "s":
                        step_s(L, s)
                    elif s[0] == "x":
                        step_x(L, s)
                    elif s[0] == "mixn":
                        step_mixn(L, s)
                for d in range(KT):
                    out_tile(L, d)
                for r in range(3):
                    gate_up(L, r, r, first=True)
                    if r == 0:
                        rstd_sum(L, 1)
                with pe.Fori(1, FT // 3) as i:
                    for r in range(3):
                        gate_up(L, i * 3 + r, r)
                gate_up(L, FT - 1, 0)
                with pe.Fori(0, KT // 3) as i:
                    for r in range(3):
                        down_tile(L, i * 3 + r, r)
                for d in range(KT // 3 * 3, KT):
                    down_tile(L, d, d % 3)

        @block.scalar
        def _(act):
            A = nc.scalar.activation
            act.wait_ge(prep, 2)
            A(tables[:, :], tables[:, :], ACT.Sin).then_inc(prep, 1)
            act.wait_ge(prep, 4)
            A(lamw[:, 2 * DEPTH:4 * DEPTH], lamw[:, 0:2 * DEPTH], ACT.Exp).then_inc(prep, 1)

            def x_tile(d, gain, parity, waits):
                xs = X[:, bass.ds(d * SEQ, SEQ)]
                nc.scalar.drain()
                waits()
                A(H[:, bass.ds(d * SEQ, SEQ)], xs, ACT.Copy, scale=gain).then_inc(h_hi.sem, 1)
                A(pbuf[:, parity * SEQ:(parity + 1) * SEQ], xs, ACT.Square).then_inc(x_sq.sem, 1)

            act.wait_ge(loaded, 7 * 16)
            act.wait_ge(xin, KT * 16)
            for k in range(KT):
                def waits(k=k):
                    if k >= 2:
                        act.wait_ge(h_ready.sem, k - 1)
                x_tile(k, gain0[:, k:k + 1], k % 2, waits)

            def norm(L, use, scale, dst, sig, before):
                act.wait_ge(t_ready.sem, t_ready.after(L, use))
                before()
                A(dst, T[T_USES.index(use) % 2][:, :], ACT.Ln, scale=scale, bias=eps).then_inc(t_act.sem, 1)
                nc.scalar.drain()
                A(dst, dst, ACT.Exp, scale=-0.5).then_inc(sig, 1)

            def step_proj(L, t):
                src = pbuf[:, (t % 2) * SEQ:(t % 2 + 1) * SEQ]
                if roped(t):
                    act.wait_ge(acc_free.sem, acc_free.after(L, ("proj", t)))
                    old = previous(rope_t, t)
                    if old is not None:
                        act.wait_ge(t_ready.sem, t_ready.after(L, ("post", old)))
                    A(SQ, src, ACT.Square).then_inc(sq_ready.sem, 1)
                elif TILES[t][1] != "v":
                    g, role = TILES[t]
                    act.wait_ge(acc_free.sem, acc_free.after(L, ("proj", t)))
                    A((kbuf[g % 2] if role == "k" else qbuf[QSLOT[g, role]])[0], src, ACT.Copy).then_inc(qk_hi.sem, 1)

            def step_post(L, t):
                g, role = TILES[t]
                use = ("post", t)
                if roped(t):
                    def before():
                        old = previous(rope_t, t)
                        if old is not None:
                            act.wait_ge(qk_ready.sem, qk_ready.after(L, old))
                    norm(L, use, 1.0 / HD, RN, rn_ready.sem, before)
                elif role == "v":
                    bank = T[T_USES.index(use) % 2][:, :].rearrange("p (j e) -> p j e", j=NB)
                    act.wait_ge(t_ready.sem, t_ready.after(L, use))
                    if GROUPS[g][0] == "diff":
                        act.wait_ge(pv_done.sem, pv_done.after(L, [s for s in pvs if s[1] < g][-1]))
                        A(vbuf[0][:, :, 0, :], bank, ACT.Copy).then_inc(t_act.sem, 1)
                    else:
                        if g:
                            act.wait_ge(pv_done.sem, pv_done.after(L, [s for s in pvs if s[1] < g][-1]))
                        else:
                            act.wait_ge(zeroed.sem, zeroed.after(L, 0))
                        A(vbuf[0][:, :, 0, 0:HD], bank[:, :, 0:HD], ACT.Copy)
                        A(vbuf[0][:, :, 1, HD:P], bank[:, :, HD:P], ACT.Copy)
                        nc.scalar.drain().then_inc(t_act.sem, 1)

            def step_z(L, g, h):
                name = ("z", g, h)
                act.wait_ge(z_ready.sem, z_ready.after(L, name))
                old = previous(heads, name)
                if old is not None:
                    act.wait_ge(w_split.sem, w_split.after(L, old))
                for b, at0, n in ZE:
                    A(E[:, at0:at0 + n], Z[b][:, 0:n], ACT.Abs)
                nc.scalar.drain()
                A(E, E, ACT.Exp, scale=-1.0)
                nc.scalar.drain()
                A(E, E, ACT.Ln, bias=one).then_inc(e_ready.sem, 1)

            def step_cum(L, g, h):
                act.wait_ge(z_ready.sem, z_ready.after(L, ("cum", g, h)))
                for b, at0, n in ZE:
                    A(E[:, at0:at0 + n], Z[b][:, 0:n], ACT.Exp)
                nc.scalar.drain().then_inc(w_exp.sem, 1)

            def step_s(L, step):
                _, g, b = step
                for u in units_of(step):
                    i = UNITS.index(u)
                    st = (i % 4) * 8
                    z = Z[i % 3]
                    act.wait_ge(negmax.sem, negmax.after(L, u))
                    if GROUPS[g][0] == "diff":
                        n = P * (b + 1)
                        e = eb[2 * (ss.index(step) % 2) + u[2]]
                        A(e[:, 0:n], z[:, 0:n], ACT.Exp, bias=stat[:, st + 2:st + 3], accum_out=stat[:, st + 4:st + 5]).then_inc(exps.sem, 1)
                    else:
                        hd, bp = b
                        e = eb[2 * (ss.index(step) % 2)]
                        A(stat[:, st + 6:st + 8], stat[:, st + 2:st + 4], ACT.Exp, bias=cur[:, C_SINK + hd:C_SINK + hd + 1])
                        for j in range(2):
                            lo = 2 * P * j + (P if bp == j == 0 else 0)
                            A(e[:, lo:2 * P * (j + 1)], z[:, lo:2 * P * (j + 1)], ACT.Exp, bias=stat[:, st + 2 + j:st + 3 + j],
                              accum_out=stat[:, st + 4 + j:st + 5 + j])
                        nc.scalar.drain().then_inc(exps.sem, 1)

            def step_x(L, step):
                g = step[1]
                act.wait_ge(t_ready.sem, t_ready.after(L, step))
                i = STEPS.index(step)
                old = [s for s in pvs if STEPS.index(s) < i]
                act.wait_ge(pv_done.sem, pv_done.after(L, old[-1]))
                bank = T[T_USES.index(step) % 2][:, :].rearrange("p (j e) -> p j e", j=NB)
                for js, q, c0, c1 in pt_parts(step):
                    A(pt[0][:, js, q * P:(q + 1) * P], bank[:, c0:c1, :], ACT.Copy)
                nc.scalar.drain().then_inc(t_act.sem, 1)

            def step_mix(L, step):
                m = mix_tile(step)
                act.wait_ge(pv_done.sem, pv_done.after(L, last_pv(step)))
                if GROUPS[step[1]][0] == "diff":
                    old = previous(mixns, ("mixn",) + step[1:])
                    if old is not None:
                        act.wait_ge(mix_ready.sem, mix_ready.after(L, mix_tile(old)))
                    A(MSQ, O[:, :], ACT.Square).then_inc(mix_act.sem, 1)
                else:
                    A(mix[0][:, m * SEQ:(m + 1) * SEQ], O[:, :], ACT.Copy).then_inc(mix_act.sem, 1)

            def gate_up(L, f, r):
                nc.scalar.drain()
                act.wait_ge(acc_free.sem, acc_free.nth(L, f * 2 + (A_GU + 1)))
                act.wait_ge(loaded, 16)
                A(gbuf[r], gbuf[r], ACT.Silu).then_inc(silu.sem, 1)

            with act.Fori(0, DEPTH) as L:
                norm(L, ("rstd", 0), 1.0 / D_MODEL, rstd[:, :], rstd_ready.sem, lambda: None)
                for s in STEPS:
                    nc.scalar.drain()
                    if s[0] == "proj":
                        step_proj(L, s[1])
                    elif s[0] == "post":
                        step_post(L, s[1])
                    elif s[0] == "z":
                        step_z(L, s[1], s[2])
                    elif s[0] == "cum":
                        step_cum(L, s[1], s[2])
                    elif s[0] == "s":
                        step_s(L, s)
                    elif s[0] == "x":
                        step_x(L, s)
                    elif s[0] == "mix":
                        step_mix(L, s)
                    elif s[0] == "mixn":
                        norm(L, s, 1.0 / P, MRN[:, :], mrn_ready.sem, lambda: None)
                for d in range(KT):
                    def waits(d=d):
                        act.wait_ge(acc_free.sem, acc_free.nth(L, A_WO + d + 1))
                    x_tile(d, cur[:, C_FG + d:C_FG + d + 1], d % 2, waits)
                norm(L, ("rstd", 1), 1.0 / D_MODEL, rstd[:, :], rstd_ready.sem, lambda: None)
                with act.Fori(0, FT // 3) as i:
                    for r in range(3):
                        gate_up(L, i * 3 + r, r)
                gate_up(L, FT - 1, 0)
                with act.Fori(0, KT // 2) as i:
                    for r in range(2):
                        d = i * 2 + r

                        def waits():
                            act.wait_ge(acc_free.sem, acc_free.nth(L, d + (A_DOWN + 1)))
                            act.wait_ge(loaded, 16)
                        x_tile(d, cur[:, bass.ds(d + C_NG, 1)], r, waits)

        @block.vector
        def _(dve):
            V = nc.vector
            drain = V.drain
            tt, ts, stt, cp = V.tensor_tensor, V.tensor_scalar, V.scalar_tensor_tensor, V.tensor_copy

            dve.wait_ge(loaded, 7 * 16)
            cp(constr[:, :], U[:, 0:2 * P])
            cp(constb[:, P:4 * P], U[:, 2 * P:5 * P])
            cp(constb[:, 0:P], ident)
            V.memset(ssum, 0.0)
            drain().then_inc(prep, 1)
            TWO_PI = 2 * np.pi
            C1 = 6.28125
            C2 = float(np.float32(TWO_PI - C1))
            C3 = float(np.float32(TWO_PI - C1 - C2))
            MAGIC = 1.5 * 2.0 ** 23
            PI = 3.1415925
            cp(work[:, 0:SEQ], pbuf[:, 0:SEQ].bitcast(I32))
            drain()
            ts(work[:, 0:SEQ], work[:, 0:SEQ], misc[:, 0:1], None, ALU.mult)
            drain()
            for i, turn in ((0, 0.25), (1, 0.0)):
                n, r = work[:, (1 + i) * SEQ:(2 + i) * SEQ], tables[:, i * SEQ:(i + 1) * SEQ]
                ts(n, work[:, 0:SEQ], 1.0 / TWO_PI, turn, ALU.mult, ALU.add)
                drain()
                ts(n, n, MAGIC, MAGIC, ALU.add, ALU.subtract)
                drain()
                stt(r, n, -C1, work[:, 0:SEQ], ALU.mult, ALU.add)
                drain()
                stt(r, n, -C2, r, ALU.mult, ALU.add)
                drain()
                stt(r, n, -C3, r, ALU.mult, ALU.add)
                drain()
                if i == 0:
                    ts(r, r, np.pi / 2, None, ALU.add)
                    drain()
                ts(r, r, PI, -PI, ALU.min, ALU.max)
            drain().then_inc(prep, 1)
            dve.wait_ge(prep, 3)
            ts(SIN, SIN, misc[:, 1:2], None, ALU.mult)
            for l in range(DEPTH):
                for i in range(2):
                    a = lam[:, (4 * l + 2 * i) * HD:(4 * l + 2 * i + 1) * HD]
                    tt(a, a, lam[:, (4 * l + 2 * i + 1) * HD:(4 * l + 2 * i + 2) * HD], ALU.mult)
                    drain()
                    V.reduce_sum(lamw[:, 2 * l + i:2 * l + i + 1], a, AX_X)
            drain().then_inc(prep, 1)
            dve.wait_ge(prep, 5)
            for l in range(DEPTH):
                o = 2 * DEPTH + 2 * l
                nl = par[:, l * NPAR + C_NLAM:l * NPAR + C_NLAM + 1]
                tt(nl, lamw[:, o + 1:o + 2], lamw[:, o:o + 1], ALU.subtract)
                drain()
                tt(nl, nl, misc[:, 4 + l:5 + l], ALU.subtract)
                g = par[:, l * NPAR + C_SUB:l * NPAR + C_SUB + 1]
                tt(g, g, misc[:, 6 + l:7 + l], ALU.mult)
                for c in (C_DQ, C_WQ):
                    g = par[:, l * NPAR + c:l * NPAR + c + 1]
                    ts(g, g, SCALE, None, ALU.mult)
            drain()

            def x_tile(d, gain, parity):
                xs = X[:, bass.ds(d * SEQ, SEQ)]
                stt(H[:, bass.ds(d * SEQ + KT * SEQ, SEQ)], xs, gain, H[:, bass.ds(d * SEQ, SEQ)].bitcast(F32),
                    ALU.mult, ALU.subtract).then_inc(h_ready.sem, 1)

            def square_sum(parity):
                return tt(ssum, ssum, pbuf[:, parity * SEQ:(parity + 1) * SEQ], ALU.add)

            for k in range(KT):
                drain()
                dve.wait_ge(x_sq.sem, k + 1)
                square_sum(k % 2)
                x_tile(k, gain0[:, k:k + 1], k % 2)
            drain().then_inc(ssum_ready.sem, 1)

            def tile_of(g, role):
                return TILES.index((g, role))

            def slot_of(t):
                g, role = TILES[t]
                if role == "k":
                    return kbuf[g % 2]
                return qbuf[QSLOT[g, role]]

            def step_proj(L, t):
                g, role = TILES[t]
                if t == 0:
                    dve.wait_ge(rstd_ready.sem, rstd_ready.after(L, 0))
                dve.wait_ge(blocks_done.sem, blocks_done.nth(L, t + 1))
                c = SCALE if role == "q0" and GROUPS[g][0] == "sb" else 1.0
                stt(pbuf[:, (t % 2) * SEQ:(t % 2 + 1) * SEQ], acc[t % 2][:, :], c, rstd[:, :], ALU.mult, ALU.mult)\
                    .then_inc(acc_free.sem, 1)

            def step_post(L, t):
                g, role = TILES[t]
                kind = GROUPS[g][0]
                src = pbuf[:, (t % 2) * SEQ:(t % 2 + 1) * SEQ]
                if roped(t):
                    hi, lo = slot_of(t)
                    gain = {"diff": {"q0": C_DQ, "k": C_DK}, "swa": {"q0": C_WQ, "q1": C_WQ, "k": C_WK}}[kind][role]
                    dve.wait_ge(rn_ready.sem, rn_ready.after(L, t))
                    stt(Y, src, cur[:, gain:gain + 1], RN, ALU.mult, ALU.mult)
                    drain()
                    V.stream_shuffle(ROT, Y, [(i + 16) % 32 for i in range(32)])
                    tt(Y, Y, COS, ALU.mult)
                    drain()
                    tt(ROT, ROT, SIN, ALU.mult)
                    drain()
                    tt(Y, Y, ROT, ALU.add)
                    drain()
                    old = [n for n in z_names if (n[1] if n[0] in ("z", "cum") else n[0]) == g - 2]
                    dve.wait_ge(z_ready.sem, z_ready.after(L, old[-1]))
                    cp(hi, Y)
                    drain()
                    tt(lo, Y, hi.bitcast(F32), ALU.subtract).then_inc(qk_ready.sem, 1)
                elif role == "v":
                    bank = T[T_USES.index(("post", t)) % 2][:, :].rearrange("p (j e) -> p j e", j=NB)
                    dve.wait_ge(t_act.sem, t_act.after(L, ("post", t)))
                    hi, lo = vbuf
                    if kind == "diff":
                        tt(lo[:, :, 0, :], bank, hi[:, :, 0, :].bitcast(F32), ALU.subtract).then_inc(t_dve.sem, 1)
                    else:
                        tt(lo[:, :, 0, 0:HD], bank[:, :, 0:HD], hi[:, :, 0, 0:HD].bitcast(F32), ALU.subtract)
                        tt(lo[:, :, 1, HD:P], bank[:, :, HD:P], hi[:, :, 1, HD:P].bitcast(F32), ALU.subtract)
                        drain().then_inc(t_dve.sem, 1)
                else:
                    hi, lo = slot_of(t)
                    dve.wait_ge(qk_hi.sem, qk_hi.after(L, t))
                    tt(lo, src, hi.bitcast(F32), ALU.subtract).then_inc(qk_ready.sem, 1)
                if t == 1:
                    V.memset(vbuf[0].bitcast(F32), 0.0)
                    V.memset(vbuf[1].bitcast(F32), 0.0)
                    drain().then_inc(zeroed.sem, 1)

            def step_z(L, g, h):
                name = ("z", g, h)
                dve.wait_ge(e_ready.sem, e_ready.after(L, name))
                for b, at0, n in ZE:
                    stt(E[:, at0:at0 + n], Z[b][:, 0:n], 0.0, E[:, at0:at0 + n], ALU.max, ALU.add)
                drain()
                cp(spb[0], E)
                drain()
                tt(spb[1], E, spb[0].bitcast(F32), ALU.subtract).then_inc(sp_ready.sem, 1)

            def step_cum(L, g, h):
                dve.wait_ge(w_exp.sem, w_exp.after(L, ("z", g, h)))
                i = STEPS.index(("cum", g, h))
                old = [s for s in pvs if STEPS.index(s) < i]
                if old:
                    dve.wait_ge(pv_done.sem, pv_done.after(L, old[-1]))
                for j in range(NB):
                    cp(pt[0][:, j, P * j:SEQ], epart(E, j))
                drain()
                for j in range(NB):
                    tt(pt[1][:, j, P * j:SEQ], epart(E, j), pt[0][:, j, P * j:SEQ].bitcast(F32), ALU.subtract)
                drain().then_inc(w_split.sem, 1)

            def step_s(L, step):
                _, g, b = step
                for u in units_of(step):
                    i = UNITS.index(u)
                    st = (i % 4) * 8
                    z = Z[i % 3]
                    dve.wait_ge(z_ready.sem, z_ready.after(L, u))
                    if GROUPS[g][0] == "diff":
                        V.reduce_max(stat[:, st:st + 1], z[:, 0:P * (b + 1)], AX_X)
                        drain()
                        ts(stat[:, st + 2:st + 3], stat[:, st:st + 1], -1.0, None, ALU.mult).then_inc(negmax.sem, 1)
                    else:
                        hd, bp = b
                        if bp == 0:
                            V.reduce_max(stat[:, st:st + 1], z[:, P:2 * P], AX_X)
                            V.reduce_max(stat[:, st + 1:st + 2], z[:, 2 * P:4 * P], AX_X)
                        else:
                            V.reduce_max(stat[:, st:st + 2], z[:, :].rearrange("p (b k) -> p b k", b=2), AX_X)
                        drain()
                        ts(stat[:, st + 2:st + 4], stat[:, st:st + 2], cur[:, C_SINK + hd:C_SINK + hd + 1], -1.0,
                           ALU.max, ALU.mult).then_inc(negmax.sem, 1)

            def step_x(L, step):
                _, g, b = step
                k = ss.index(("s", g, b))
                us = [u for u in UNITS if u[0] == g and u[1] == b]
                dve.wait_ge(exps.sem, exps.after(L, us[-1]))
                if k >= 2:
                    dve.wait_ge(t_ready.sem, t_ready.after(L, ("x",) + ss[k - 2][1:]))
                dst = at[k % 2]
                if GROUPS[g][0] == "diff":
                    n = P * (b + 1)
                    s0, s1 = ((UNITS.index(u) % 4) * 8 for u in us)
                    e0, e1 = eb[2 * (k % 2)], eb[2 * (k % 2) + 1]
                    V.reciprocal(stat[:, s0 + 5:s0 + 6], stat[:, s0 + 4:s0 + 5])
                    V.reciprocal(stat[:, s1 + 5:s1 + 6], stat[:, s1 + 4:s1 + 5])
                    drain()
                    ts(e1[:, 0:n], e1[:, 0:n], stat[:, s1 + 5:s1 + 6], cur[:, C_NLAM:C_NLAM + 1], ALU.mult, ALU.mult)
                    drain()
                    stt(dst[:, 0:n], e0[:, 0:n], stat[:, s0 + 5:s0 + 6], e1[:, 0:n], ALU.mult, ALU.add).then_inc(at_ready.sem, 1)
                else:
                    st = (UNITS.index(us[0]) % 4) * 8
                    e = eb[2 * (k % 2)]
                    tt(stat[:, st + 4:st + 6], stat[:, st + 4:st + 6], stat[:, st + 6:st + 8], ALU.add)
                    drain()
                    V.reciprocal(stat[:, st + 6:st + 8], stat[:, st + 4:st + 6])
                    drain()
                    for j in range(2):
                        lo = 2 * P * j + (P if b[1] == j == 0 else 0)
                        ts(dst[:, lo:2 * P * (j + 1)], e[:, lo:2 * P * (j + 1)], stat[:, st + 6 + j:st + 7 + j], None, ALU.mult)
                    drain().then_inc(at_ready.sem, 1)
                dve.wait_ge(t_act.sem, t_act.after(L, step))
                bank = T[T_USES.index(step) % 2][:, :].rearrange("p (j e) -> p j e", j=NB)
                for js, q, c0, c1 in pt_parts(step):
                    tt(pt[1][:, js, q * P:(q + 1) * P], bank[:, c0:c1, :], pt[0][:, js, q * P:(q + 1) * P].bitcast(F32), ALU.subtract)
                drain().then_inc(t_dve.sem, 1)

            def step_mix(L, step):
                if GROUPS[step[1]][0] == "diff":
                    return
                m = mix_tile(step)
                cols = slice(m * SEQ, (m + 1) * SEQ)
                dve.wait_ge(mix_act.sem, mix_act.after(L, step))
                tt(mix[1][:, cols], O[:, :], mix[0][:, cols].bitcast(F32), ALU.subtract).then_inc(mix_ready.sem, 1)

            def step_mixn(L, step):
                m = mix_tile(step)
                cols = slice(m * SEQ, (m + 1) * SEQ)
                dve.wait_ge(mrn_ready.sem, mrn_ready.after(L, step))
                stt(MRN[:, :], O[:, :], cur[:, C_SUB:C_SUB + 1], MRN[:, :], ALU.mult, ALU.mult)
                drain()
                cp(mix[0][:, cols], MRN[:, :])
                drain()
                tt(mix[1][:, cols], MRN[:, :], mix[0][:, cols].bitcast(F32), ALU.subtract).then_inc(mix_ready.sem, 1)

            def gate_up(L, f, r):
                g, u = gubank[2 * r], gubank[2 * r + 1]
                drain()
                dve.wait_ge(rstd_ready.sem, rstd_ready.after(L, 1))
                dve.wait_ge(blocks_done.sem, blocks_done.nth(L, f * 2 + (A_GU + 1)))
                tt(gbuf[r], g[:, :], rstd[:, :], ALU.mult).then_inc(acc_free.sem, 1)
                dve.wait_ge(blocks_done.sem, blocks_done.nth(L, f * 2 + (A_GU + 2)))
                tt(ubuf[r], u[:, :], rstd[:, :], ALU.mult).then_inc(acc_free.sem, 1)
                drain()
                dve.wait_ge(silu.sem, silu.nth(L, f + 1))
                tt(ubuf[r], ubuf[r], gbuf[r], ALU.mult)
                drain()
                cp(ff[0][:, bass.ds(f * SEQ, SEQ)], ubuf[r])
                drain()
                tt(ff[1][:, bass.ds(f * SEQ, SEQ)], ubuf[r], ff[0][:, bass.ds(f * SEQ, SEQ)].bitcast(F32), ALU.subtract)\
                    .then_inc(ffr.sem, 1)

            def x_stage_tile(L, blocks, n0, d, bank, gain, r):
                xs = X[:, bass.ds(d * SEQ, SEQ)]
                drain()
                dve.wait_ge(blocks_done.sem, blocks_done.nth(L, blocks))
                tt(xs, xs, bank[:, :], ALU.add).then_inc(acc_free.sem, 1)
                drain()
                dve.wait_ge(x_sq.sem, x_sq.nth(L, d + (n0 + 1)))
                square_sum(r)
                x_tile(d, gain, r)

            with dve.Fori(0, DEPTH) as L:
                cp(cur[:, :], par[:, bass.ds(L * NPAR, NPAR)])
                drain()
                for s in STEPS:
                    drain()
                    if s[0] == "proj":
                        step_proj(L, s[1])
                    elif s[0] == "post":
                        step_post(L, s[1])
                    elif s[0] == "z":
                        step_z(L, s[1], s[2])
                    elif s[0] == "cum":
                        step_cum(L, s[1], s[2])
                    elif s[0] == "s":
                        step_s(L, s)
                    elif s[0] == "x":
                        step_x(L, s)
                    elif s[0] == "mix":
                        step_mix(L, s)
                    elif s[0] == "mixn":
                        step_mixn(L, s)
                V.memset(ssum, 0.0)
                drain()
                for d in range(KT):
                    x_stage_tile(L, NT + d + 1, 0, d, acc[d % 2], cur[:, C_FG + d:C_FG + d + 1], d % 2)
                drain().then_inc(ssum_ready.sem, 1)
                with dve.Fori(0, FT // 3) as i:
                    for r in range(3):
                        gate_up(L, i * 3 + r, r)
                gate_up(L, FT - 1, 0)
                V.memset(ssum, 0.0)
                drain()
                for d in range(KT):
                    x_stage_tile(L, N8 + 2 * d + 2, KT, d, downbank[d % 3], cur[:, C_NG + d:C_NG + d + 1], d % 2)
                drain().then_inc(ssum_ready.sem, 1)


def _launch_layout(inputs):
    f32 = np.float32
    g = {k: np.asarray(v) for k, v in inputs.items()}
    perm = np.concatenate([np.arange(0, 16), np.arange(32, 48), np.arange(16, 32), np.arange(48, 64)])
    perm2 = np.concatenate([perm, HD + perm])
    sbw, dqk, dw = 256, 512, 512
    o_sq, o_sk, o_sv = 0, sbw, 2 * sbw
    o_dq, o_dk, o_dv = 3 * sbw, 3 * sbw + dqk, 3 * sbw + 2 * dqk
    o_wq = o_dv + dw
    o_wk, o_wv = o_wq + 256, o_wq + 256 + 128
    cols = []
    for (grp, role) in TILES:
        kind, i = GROUPS[grp]
        if kind == "sb":
            cols.append({"q0": o_sq, "k": o_sk, "v": o_sv}[role] + i * P + np.arange(P))
        elif kind == "diff":
            cols.append({"q0": o_dq, "k": o_dk, "v": o_dv}[role] + i * P + (np.arange(P) if role == "v" else perm2))
        elif role[0] == "q":
            t = int(role[1])
            cols.append(o_wq + np.concatenate([t * HD + perm, (t + 2) * HD + perm]))
        else:
            cols.append({"k": o_wk + perm2, "v": o_wv + np.arange(P)}[role])
    cols = np.concatenate(cols)
    c0 = sbw + dw
    rows = np.concatenate([np.arange(sbw)] + [c0 + h * HD + np.arange(HD) for h in (0, 2, 1, 3)] + [sbw + np.arange(dw)])

    def blocks(w):
        return w.reshape(w.shape[0] // P, P, w.shape[1] // P, P).transpose(2, 1, 0, 3)
    w8, w11 = [], []
    for l in range(DEPTH):
        w8.append(blocks(g["w_in"][l][:, cols]))
        w8.append(blocks(g["w_o"][l][rows]))
        gu = np.stack([blocks(g["w_gate"][l]), blocks(g["w_up"][l])], axis=1)
        w8.append(gu.reshape(2 * FT, P, KT, P))
        w11.append(blocks(g["w_down"][l]).reshape(KT, P, 2, HALF, P).transpose(0, 2, 1, 3, 4).reshape(N11, P, HALF, P))
    w8 = np.concatenate(w8).reshape(DEPTH * N8, P, KT * P)
    w11 = np.concatenate(w11).reshape(DEPTH * N11, P, HALF * P)
    par = [g["attn_norm_g"][0].reshape(KT, P).T]
    for l in range(DEPTH):
        two = lambda v: np.concatenate([v[l][perm], v[l][perm]])[:, None]
        nxt = g["attn_norm_g"][(l + 1) % DEPTH]
        par += [g["ffn_norm_g"][l].reshape(KT, P).T, nxt.reshape(KT, P).T,
                two(g["diff_q_norm_g"]), two(g["diff_k_norm_g"]), two(g["swa_q_norm_g"]), two(g["swa_k_norm_g"]),
                g["diff_subln_g"][l][:, None],
                np.tile(g["swa_sinks"][l][[0, 2, 1, 3]][None, :], (P, 1)), np.zeros((P, 1), f32)]
    par = np.concatenate(par, axis=1)
    lam = np.tile(g["diff_lambda"].reshape(1, -1), (P, 1))
    misc = np.zeros((P, 8), f32)
    inv = f32(1) / f32(ROPE_THETA) ** (np.arange(0, HD, 2, dtype=f32) / f32(HD))
    misc[:, 0] = inv[perm2 % HD % 32]
    misc[:, 1] = np.where(perm2 % HD < 32, -1.0, 1.0)
    misc[:, 2] = EPS
    misc[:, 3] = 1.0
    for l in range(DEPTH):
        li = 0.8 - 0.6 * np.exp(-0.3 * l)
        misc[:, 4 + l], misc[:, 6 + l] = li, 1.0 - li
    i, j = np.arange(P)[:, None], np.arange(P)[None, :]
    const = np.zeros((P, NCONST), f32)
    const[:, K_ID:K_ID + P] = i == j
    const[:, K_BLK:K_BLK + P] = i // HD == j // HD
    const[:, K_ONE:K_ONE + P] = 1.0
    const[:, K_TRI:K_TRI + P] = -1.0 * (i >= j)
    const[:, K_NEG1:K_NEG1 + P] = -1.0
    const[:, K_MSB:K_MSB + P] = NEG * (i >= j)
    const[:, K_MSW:K_MSW + P] = NEG * ((j < CHUNK) | (i >= CHUNK))
    const[:, K_MDF:K_MDF + P] = NEG * ((i < CHUNK) & (j >= CHUNK))
    x = g["x"].reshape(SEQ, KT, P).transpose(1, 2, 0)
    pos = np.tile(g["positions"].reshape(1, SEQ), (P, 1))
    return [("x", x), ("pos", pos), ("w8", w8), ("w11", w11), ("par", par), ("lam", lam), ("misc", misc), ("const", const)]


def kernel(**inputs):
    import concourse.bacc as _bacc
    from concourse.bass_utils import run_bass_kernel_spmd as _run

    nc = _bacc.Bacc("TRN2", target_bir_lowering=False, num_devices=1, dynamic_dma_scratch_size=1024)
    arrays, args = {}, []
    for name, a in _launch_layout(inputs):
        a = np.ascontiguousarray(a)
        arrays[f"in_{name}"] = a
        args.append(nc.dram_tensor(f"in_{name}", a.shape, mybir.dt.from_np(a.dtype), kind="ExternalInput").ap())
    out = nc.dram_tensor("out_x", (KT, P, SEQ), F32, kind="ExternalOutput").ap()
    trunk_kernel(nc, *args, out)
    r = _run(nc, [arrays], core_ids=[0])
    y = r.results[0]["out_x"]
    return np.ascontiguousarray(y.transpose(2, 0, 1).reshape(1, SEQ, D_MODEL))
```

```python
from contextlib import ExitStack

import concourse.bass as bass
import numpy as np
from concourse import mybir

F32 = mybir.dt.float32
F32R = mybir.dt.float32r
BF16 = mybir.dt.bfloat16
I32 = mybir.dt.int32
ACT = mybir.ActivationFunctionType
ALU = mybir.AluOpType
AX_X = mybir.AxisListType.X

P = 128
D_MODEL = 1024
SEQ = 512
DEPTH = 2
HD = 64
CHUNK = 64
ROPE_THETA = 10000.0
EPS = 1e-6
D_FF = -(-8 * D_MODEL // (3 * 256)) * 256
SCALE = HD ** -0.5
KT = D_MODEL // P
FT = D_FF // P
NB = SEQ // P
NEG = -1e30

GROUPS = [("sb", 0), ("sb", 1), ("swa", 0), ("diff", 0), ("diff", 1), ("diff", 2), ("diff", 3)]
TILES = []
for _g, (_kind, _i) in enumerate(GROUPS):
    for _role in (["q0", "q1", "k", "v"] if _kind == "swa" else ["q0", "k", "v"]):
        TILES.append((_g, _role))
NT = len(TILES)
QSLOT = {(0, "q0"): 0, (1, "q0"): 1, (2, "q0"): 0, (2, "q1"): 2, (3, "q0"): 1, (4, "q0"): 0, (5, "q0"): 1, (6, "q0"): 0}

HALF = FT // 2
N8 = NT + KT + 2 * FT
N11 = 2 * KT
WPER = N8 + N11
RING = 3
assert WPER % RING == 0 and (NT + KT) % RING == 0
A_WO, A_GU, A_DOWN = NT, NT + KT, NT + KT + 2 * FT
ACCS = A_DOWN + KT

C_FG, C_NG, C_DQ, C_DK, C_WQ, C_WK, C_SUB, C_SINK, C_NLAM, NPAR = 0, 8, 16, 17, 18, 19, 20, 21, 25, 26
K_ID, K_BLK, K_ONE, K_TRI, K_NEG1, K_MSB, K_MSW, K_MDF, NCONST = (P * i for i in range(9))


class Signal:

    def __init__(self, sem, events, before=0):
        self.sem, self.before = sem, before
        self.count = {e: i + 1 for i, e in enumerate(events)}
        self.per = len(events)

    def after(self, L, event):
        return L * self.per + (self.before + self.count[event])

    def nth(self, L, n):
        return L * self.per + (n + self.before)


def attention_steps():
    within = ["ws", "pv", "s", "z", "cum", "x", "mix", "mixn", "ms", "vt", "ev", "xl", "mixl", "sp", "ra", "rb",
              "c", "rl", "vl", "proj", "rstd"]
    placed = []

    def place(slot, *step):
        placed.append((slot, within.index(step[0]), len(placed), step))

    place(1, "rstd", 0)
    for t, (g, role) in enumerate(TILES):
        place(2 * t, "proj", t, 0)
        place(2 * t + 1, "proj", t, 1)
        place(2 * t + 2, "ev", t)
        if role == "v":
            place(2 * t + 3, "vt", t)
            place(2 * t + 3, "vl", t)
        elif roped(t):
            place(2 * t + 3, "ms", t)
            place(2 * t + 3, "ra", t)
            place(2 * t + 4, "rb", t)
            place(2 * t + 4, "rl", t)
        else:
            place(2 * t + 3, "rl", t)
    for g, a in ((0, 6), (1, 13)):
        for h in range(2):
            for i, kind in enumerate(("z", "sp", "cum", "ws", "pv")):
                place(a + 3 * h + i, kind, g, h)
        place(a + 8, "mix", g, 0)
        place(a + 8, "mixl", g, 0)
    for hd, a in enumerate((21, 22, 24, 25)):
        for half in range(2):
            for i, kind in ((0, "s"), (0, "c"), (1, "x"), (1, "xl")):
                place(a + i, kind, 2, (hd, half))
        place(a + 2, "pv", 2, hd)
        if hd % 2:
            place(a + 3, "mix", 2, hd // 2)
            place(a + 3, "mixl", 2, hd // 2)
    for g, a in ((3, 27), (4, 33), (5, 39), (6, 45)):
        for b in range(NB):
            for i, kind in ((0, "s"), (0, "c"), (1, "x"), (1, "xl")):
                place(a + b + i, kind, g, b)
        place(a + 5, "pv", g, 0)
        for i, kind in ((6, "mix"), (7, "mixn"), (7, "mixl")):
            place(a + i, kind, g, 0)
    return [p[3] for p in sorted(placed)]


def roped(t):
    return GROUPS[TILES[t][0]][0] != "sb" and TILES[t][1] != "v"


STEPS = attention_steps()
T_USES = [s for s in STEPS if s[0] in ("rstd", "x", "mixn", "ms", "vt")] + [("rstd", 1)]
LO_OF = {"x": "xl", "vt": "vl"}


def steps(*kinds):
    return [s for s in STEPS if s[0] in kinds]


def before(step, *kinds):
    found = [s for s in STEPS[:STEPS.index(step)] if s[0] in kinds]
    return found[-1] if found else None


def mix_tile(g, i):
    return {"sb": g, "swa": 2 + i, "diff": g + 1}[GROUPS[g][0]]


def banks_of(step):
    if step[0] == "z":
        return [0, 1, 2]
    k = steps("s").index(step) % 3
    return [k] if GROUPS[step[1]][0] == "swa" else [[0, 1], [0, 2], [1, 2]][k]


def trunk_kernel(nc, x_in, pos_in, w8_in, w11_in, par_in, lam_in, misc_in, const_in, out):
    ctx = ExitStack()
    with ctx:
        def sb(name, cols, dt=F32):
            return ctx.enter_context(nc.sbuf_tensor(name, [P, cols], dt))

        def sem(name):
            return ctx.enter_context(nc.semaphore(name))

        X = sb("X", KT * SEQ)
        H = sb("H", 2 * KT * SEQ, F32R)
        raw = sb("raw", RING * HALF * P)
        W = sb("W", RING * 2 * HALF * P, F32R)
        R = sb("R", 2 * FT * SEQ, F32R)
        tables = sb("tables", 2 * SEQ)
        pbuf = sb("pbuf", 2 * SEQ)
        work = sb("work", 4 * SEQ)
        MRN = sb("MRN", SEQ)
        U = sb("U", 6 * SEQ)
        rstd = sb("rstd", SEQ)
        par = sb("par", DEPTH * NPAR)
        gain0 = sb("gain0", KT)
        cur = sb("cur", NPAR)
        lam = MRN[:, 0:DEPTH * 4 * HD]
        lamw = sb("lamw", 8 * DEPTH)
        misc = sb("misc", 8)
        const = sb("const", 3 * P)
        constr = sb("constr", 2 * P, F32R)
        constb = sb("constb", 4 * P, BF16)
        stat = sb("stat", 32)
        idle = sb("idle", 2)

        def rpart(at, n):
            return R[:, at * SEQ:(at + n) * SEQ]
        mix = [rpart(0, KT), rpart(KT, KT)]
        qbuf = [[rpart(16 + 2 * s, 1), rpart(17 + 2 * s, 1)] for s in range(2)] + [[rpart(41, 1), rpart(42, 1)]]
        kbuf = [[rpart(20 + 2 * s, 1), rpart(21 + 2 * s, 1)] for s in range(2)]
        vbuf = [rpart(24 + 2 * s, 2).rearrange("p (j a e) -> p j a e", j=NB, a=2) for s in range(2)]
        pt = [rpart(28 + 4 * s, 4).rearrange("p (j q) -> p j q", j=NB) for s in range(2)]
        spb = [R[:, 36 * SEQ:36 * SEQ + 1280], R[:, 36 * SEQ + 1280:36 * SEQ + 2560]]
        ff = [rpart(0, FT), rpart(FT, FT)]
        SQ, RN, Y, ROT = (work[:, i * SEQ:(i + 1) * SEQ] for i in range(4))
        ssum = ROT
        COS, SIN = tables[:, 0:SEQ], tables[:, SEQ:2 * SEQ]
        E = U[:, 0:1280]
        eb = [U[:, i * SEQ:(i + 1) * SEQ] for i in range(4)]
        at = [U[:, (4 + i) * SEQ:(5 + i) * SEQ] for i in range(2)]
        gbuf = [U[:, i * SEQ:(i + 1) * SEQ] for i in range(3)]
        ubuf = [U[:, (3 + i) * SEQ:(4 + i) * SEQ] for i in range(3)]
        ident, blk, ones = (const[:, i * P:(i + 1) * P] for i in range(3))
        tri, neg1 = constr[:, 0:P], constr[:, P:2 * P]
        identb, msb = constb[:, 0:P], constb[:, P:2 * P]
        msw, mdf = constb[:, 2 * P:4 * P], constb[:, 3 * P:4 * P]
        eps, one = misc[:, 2:3], misc[:, 3:4]

        banks = [ctx.enter_context(nc.psum_tensor(f"bank{i}", [P, 512], F32)) for i in range(2)]
        zall = ctx.enter_context(nc.psum_tensor("scores", [P, 3 * 512], F32))
        Z = [zall[:, 512 * i:512 * (i + 1)] for i in range(3)]
        banks += Z + [ctx.enter_context(nc.psum_tensor(f"bank{i}", [P, 512], F32)) for i in range(5, 8)]
        acc, O, T = banks[0:2], banks[5], banks[6:8]
        gubank = banks[0:6]
        downbank = banks[2:5]
        zreg = [(0, 0, 512), (1, 0, 384), (2, 0, 256), (1, 384, 128)]
        eoff = [0, 512, 1024, 896]

        def zpart(j, skip=0):
            b, c, n = zreg[j]
            return Z[b][:, c + skip:c + n]

        def epart(buf, j):
            return buf[:, eoff[j]:eoff[j] + SEQ - P * j]
        ZE = [(0, 0, 512), (1, 512, 512), (2, 1024, 256)]

        loaded, xin = sem("loaded"), sem("x_loaded")
        prep = sem("prepared")
        raw_ready = [sem(f"raw_ready{s}") for s in range(RING)]
        w_hi = sem("w_hi_done")
        out_done = sem("out_done")
        tiles8 = [("wo", d) for d in range(KT)] + [("down", d) for d in range(KT)]
        acc_names = [("ev", t) for t in range(NT)] + [("wo", d) for d in range(KT)] + [(r, f) for f in range(FT) for r in "gu"] + [("down", d) for d in range(KT)]
        w_ready = Signal(sem("w_ready"), range(WPER), before=RING)
        blocks_done = Signal(sem("blocks_done"), range(WPER), before=RING)
        acc_free = Signal(sem("acc_free"), acc_names)
        t_ready = Signal(sem("t_ready"), T_USES)
        t_act = Signal(sem("t_read_act"), T_USES)
        t_dve = Signal(sem("t_read_dve"), steps(*LO_OF.values()))
        z_ready = Signal(sem("z_ready"), steps("z", "cum", "s"))
        pv_done = Signal(sem("pv_done"), steps("pv"))
        ln_ready = Signal(sem("ln_ready"), steps("z"))
        sp_ready = Signal(sem("softplus_ready"), steps("sp"))
        w_exp = Signal(sem("weights_exp"), steps("cum"))
        w_split = Signal(sem("weights_split"), steps("ws"))
        negmax = Signal(sem("negmax_ready"), steps("s"))
        exps = Signal(sem("exp_ready"), steps("s"))
        at_ready = Signal(sem("probs_ready"), steps("c"))
        sq_ready = Signal(sem("squares_ready"), [s for s in steps("ev") if roped(s[1])])
        rn_ready = Signal(sem("headnorm_ready"), steps("ms"))
        rotated = Signal(sem("rotated"), steps("rb"))
        qk_hi = Signal(sem("qk_hi_ready"), [("rl", s[1]) for s in STEPS if s[0] == "rb" or (s[0] == "ev" and not roped(s[1]) and TILES[s[1]][1] != "v")])
        qk_ready = Signal(sem("qk_ready"), steps("rl"))
        mix_act = Signal(sem("mix_act"), steps("mix"))
        mrn_ready = Signal(sem("mixnorm_ready"), steps("mixn"))
        mix_ready = Signal(sem("mix_ready"), range(KT))
        h_hi = Signal(sem("h_hi_ready"), tiles8, before=KT)
        x_sq = Signal(sem("x_squares"), tiles8, before=KT)
        h_ready = Signal(sem("h_ready"), tiles8, before=KT)
        ssum_ready = Signal(sem("ssum_ready"), ["wo", "down"], before=1)
        rstd_ready = Signal(sem("rstd_ready"), [("rstd", 0), ("rstd", 1)])
        silu = Signal(sem("silu_ready"), range(FT))
        zeroed = Signal(sem("values_zeroed"), [0])
        ffr = Signal(sem("ff_ready"), range(FT))

        block = ctx.enter_context(nc.Block())

        def pt_parts(step):
            _, g, b = step
            if GROUPS[g][0] == "diff":
                return [(slice(0, b + 1), b, 0, b + 1)]
            out_ = []
            for i in range(2):
                bb = 2 * b[1] + i
                j0 = max(bb - 1, 0)
                out_.append((slice(j0, bb + 1), bb, 2 * i + (1 if bb == 0 else 0), 2 * i + 2))
            return out_

        def exp_columns(g, b, i):
            k = 2 * (steps("s").index(("s", g, b)) % 2)
            if GROUPS[g][0] == "diff":
                return 0, P * (b + 1), eb[k + i]
            return 2 * P * i + (P if b[1] == i == 0 else 0), 2 * P * (i + 1), eb[k]

        def qk_buffer(g, role):
            return kbuf[g % 2] if role == "k" else qbuf[QSLOT[g, role]]

        @block.sync
        def _(sp):
            for k in range(KT):
                sp.dma_start(X[:, k * SEQ:(k + 1) * SEQ], x_in[k]).then_inc(xin, 16)
            sp.dma_start(par[:, :], par_in[:, KT:]).then_inc(loaded, 16)
            sp.dma_start(gain0[:, :], par_in[:, 0:KT]).then_inc(loaded, 16)
            sp.dma_start(misc[:, :], misc_in).then_inc(loaded, 16)
            sp.dma_start(const[:, :], const_in[:, 0:3 * P]).then_inc(loaded, 16)
            sp.dma_start(U[:, 0:NCONST - 3 * P], const_in[:, 3 * P:NCONST]).then_inc(loaded, 16)
            sp.dma_start(lam, lam_in).then_inc(loaded, 16)
            sp.dma_start(pbuf[:, 0:SEQ].bitcast(I32), pos_in).then_inc(loaded, 16)

            def load(L, n, src, cols, slot):
                sp.wait_ge(w_ready.sem, L * WPER + (n + 1))
                sp.dma_start(raw[:, slot * HALF * P:slot * HALF * P + cols], src).then_inc(raw_ready[slot], 16)

            with sp.Fori(0, DEPTH) as L:
                with sp.Fori(0, N8 // RING) as i:
                    for s in range(RING):
                        load(L, i * RING + s, w8_in[bass.ds(L * N8 + i * RING + s, 1)].rearrange("o p c -> p (o c)"), KT * P, s)
                for n in range(N8 // RING * RING, N8):
                    load(L, n, w8_in[bass.ds(L * N8 + n, 1)].rearrange("o p c -> p (o c)"), KT * P, n % RING)
                load(L, N8, w11_in[bass.ds(L * N11, 1)].rearrange("o p c -> p (o c)"), HALF * P, N8 % RING)
                with sp.Fori(0, (N11 - 1) // RING) as i:
                    for s in range(RING):
                        n = i * RING + s + 1
                        load(L, n + N8, w11_in[bass.ds(L * N11 + n, 1)].rearrange("o p c -> p (o c)"), HALF * P, (N8 + 1 + s) % RING)
            for d in range(KT):
                sp.wait_ge(acc_free.sem, acc_free.after(DEPTH - 1, ("down", d)))
                sp.dma_start(out[d], X[:, d * SEQ:(d + 1) * SEQ]).then_inc(out_done, 16)
            sp.wait_ge(out_done, 16 * KT)

        @block.gpsimd
        def _(pool):
            nc.gpsimd.memset(idle[:, 0:1], 0.0).then_inc(w_ready.sem, RING)
            pool.wait_ge(w_ready.sem, RING)

            def split(L, n, turn, cols, slot):
                src = raw[:, slot * HALF * P:slot * HALF * P + cols]
                hi = W[:, 2 * slot * HALF * P:2 * slot * HALF * P + cols]
                lo = W[:, (2 * slot + 1) * HALF * P:(2 * slot + 1) * HALF * P + cols]
                pool.wait_ge(blocks_done.sem, L * WPER + (n + 1))
                pool.wait_ge(raw_ready[slot], L * (16 * WPER // RING) + (turn + 1) * 16)
                nc.gpsimd.tensor_tensor(idle[:, 1:2], idle[:, 0:1], idle[:, 0:1], ALU.mult)
                nc.gpsimd.tensor_scalar(hi, src, 1.0, None, ALU.mult).then_inc(w_hi, 1)
                pool.wait_ge(w_hi, L * WPER + (n + 1))
                nc.gpsimd.tensor_tensor(lo, src, hi.bitcast(F32), ALU.subtract).then_inc(w_ready.sem, 1)

            with pool.Fori(0, DEPTH) as L:
                with pool.Fori(0, N8 // RING) as i:
                    for s in range(RING):
                        split(L, i * RING + s, i, KT * P, s)
                for n in range(N8 // RING * RING, N8):
                    split(L, n, n // RING, KT * P, n % RING)
                split(L, N8, N8 // RING, HALF * P, N8 % RING)
                with pool.Fori(0, (N11 - 1) // RING) as i:
                    for s in range(RING):
                        n0 = N8 + 1 + s
                        split(L, i * RING + n0, i + n0 // RING, HALF * P, n0 % RING)

        @block.tensor
        def _(pe):
            def whalf(slot, part, k):
                at0 = (2 * slot + part) * HALF * P + k * P
                return W[:, at0:at0 + P]

            def three(out_, a, b, first, last, **kw):
                nc.tensor.matmul(out_, a[0], b[0], start=first, stop=False, **kw)
                nc.tensor.matmul(out_, a[0], b[1], start=False, stop=False, **kw)
                return nc.tensor.matmul(out_, a[1], b[0], start=False, stop=last, **kw)

            def wblock(L, n, slot, out_, rhs, ks, first, last):
                pe.wait_ge(w_ready.sem, w_ready.nth(L, n + 1))
                for i, k in enumerate(ks):
                    mm = three(out_, (whalf(slot, 0, i), whalf(slot, 1, i)),
                               (rhs[0][:, k * SEQ:(k + 1) * SEQ], rhs[1][:, k * SEQ:(k + 1) * SEQ]),
                               first and i == 0, last and i == len(ks) - 1)
                return mm

            Hs = [H[:, 0:KT * SEQ], H[:, KT * SEQ:2 * KT * SEQ]]

            def t_bank(L, use):
                u = T_USES.index(use)
                if u >= 2:
                    old = T_USES[u - 2]
                    pe.wait_ge(t_act.sem, t_act.after(L, old))
                    if old[0] in LO_OF:
                        pe.wait_ge(t_dve.sem, t_dve.after(L, (LO_OF[old[0]],) + old[1:]))
                return T[u % 2]

            def take_z(L, step):
                for b in banks_of(step):
                    if b in z_owner:
                        old = z_owner[b]
                        if old[0] == "z":
                            pe.wait_ge(w_exp.sem, w_exp.after(L, ("cum",) + old[1:]))
                        else:
                            pe.wait_ge(exps.sem, exps.after(L, old))
                    z_owner[b] = step

            z_owner = {}

            def rstd_sum(L, n):
                bank = t_bank(L, ("rstd", n))
                pe.wait_ge(ssum_ready.sem, L * 2 + (n + 1))
                nc.tensor.matmul(bank[:, :], ones, ssum, start=True, stop=True).then_inc(t_ready.sem, 1)

            def step_proj(L, t, half):
                if half == 0:
                    if t >= 2:
                        pe.wait_ge(acc_free.sem, acc_free.after(L, ("ev", t - 2)))
                    pe.wait_ge(w_ready.sem, w_ready.nth(L, t + 1))
                for k in range(half * KT // 2, (half + 1) * KT // 2):
                    if t == 0:
                        pe.wait_ge(h_ready.sem, L * 16 + (k + 1))
                    mm = three(acc[t % 2][:, :], (whalf(t % RING, 0, k), whalf(t % RING, 1, k)),
                               (Hs[0][:, k * SEQ:(k + 1) * SEQ], Hs[1][:, k * SEQ:(k + 1) * SEQ]), k == 0, k == KT - 1)
                if half == 1:
                    mm.then_inc(blocks_done.sem, 1)

            def step_ms(L, t):
                bank = t_bank(L, ("ms", t))
                pe.wait_ge(sq_ready.sem, sq_ready.after(L, ("ev", t)))
                nc.tensor.matmul(bank[:, :], blk, SQ, start=True, stop=True).then_inc(t_ready.sem, 1)

            def step_vt(L, t):
                bank = t_bank(L, ("vt", t))
                pe.wait_ge(acc_free.sem, acc_free.after(L, ("ev", t)))
                for j in range(NB):
                    mm = nc.tensor.transpose(bank[:, j * P:(j + 1) * P], pbuf[:, (t % 2) * SEQ + j * P:(t % 2) * SEQ + (j + 1) * P], ident)
                mm.then_inc(t_ready.sem, 1)

            def tile_of(g, role):
                return TILES.index((g, role))

            def step_z(L, g, h):
                pe.wait_ge(qk_ready.sem, qk_ready.after(L, ("rl", tile_of(g, "k"))))
                take_z(L, ("z", g, h))
                r = slice(HD * h, HD * h + HD)
                q, k = qbuf[QSLOT[g, "q0"]], kbuf[g % 2]
                for j in range(NB):
                    keys, qs = slice(P * j, P * j + P), slice(P * j, SEQ)
                    nc.tensor.matmul(zpart(j), k[0][r, keys], q[0][r, qs], start=j < 3, stop=False, skip_group_check=True)
                    nc.tensor.matmul(zpart(j)[:, 0:P], identb, msb, start=False, stop=False, skip_group_check=True)
                    nc.tensor.matmul(zpart(j), k[0][r, keys], q[1][r, qs], start=False, stop=False, skip_group_check=True)
                    mm = nc.tensor.matmul(zpart(j), k[1][r, keys], q[0][r, qs], start=False, stop=True, skip_group_check=True)
                mm.then_inc(z_ready.sem, 1)

            def step_cum(L, g, h):
                pe.wait_ge(sp_ready.sem, sp_ready.after(L, ("sp", g, h)))
                for j in range(NB):
                    for i in range(NB - 1, j - 1, -1):
                        for part in range(2):
                            mm = nc.tensor.matmul(zpart(j, P * (i - j)), tri if i == j else neg1, epart(spb[part], i),
                                                  start=False, stop=(i == j and part == 1), skip_group_check=True)
                mm.then_inc(z_ready.sem, 1)

            def step_pv(L, g, h):
                kind = GROUPS[g][0]
                start = kind == "diff" or h % 2 == 0
                m = mix_tile(g, h // 2)
                if start and m:
                    pe.wait_ge(mix_ready.sem, mix_ready.after(L, m - 1))
                pe.wait_ge(t_dve.sem, t_dve.after(L, ("vl", tile_of(g, "v"))))
                if kind == "sb":
                    pe.wait_ge(w_split.sem, w_split.after(L, ("ws", g, h)))
                else:
                    pe.wait_ge(t_dve.sem, t_dve.after(L, ("xl", g, NB - 1 if kind == "diff" else (h, 1))))
                half = 0 if kind == "diff" else h % 2
                end = kind == "diff" or h % 2 == 1
                for j in range(NB):
                    qs = slice(P * j, min(P * (j + 2), SEQ) if kind == "swa" else SEQ)
                    vv = (vbuf[0][:, j, half, :], vbuf[1][:, j, half, :])
                    pp = (pt[0][:, j, qs], pt[1][:, j, qs])
                    mm = three(O[:, qs], vv, pp, start and j == 0, end and j == NB - 1, skip_group_check=True)
                mm.then_inc(pv_done.sem, 1)

            def step_s(L, g, b):
                kind = GROUPS[g][0]
                take_z(L, ("s", g, b))
                base = [512 * i for i in banks_of(("s", g, b))]
                if kind == "swa":
                    base.append(base[0] + 2 * P)
                kk = kbuf[g % 2]
                pe.wait_ge(qk_ready.sem, qk_ready.after(L, ("rl", tile_of(g, "k"))))
                parts = []
                for i in range(2):
                    if kind == "diff":
                        q, r = qbuf[QSLOT[g, "q0"]], slice(HD * i, HD * i + HD)
                        o = zall[:, base[i]:base[i] + P * (b + 1)]
                        parts.append((slice(P * b, P * b + P), slice(0, P * (b + 1)), o, o[:, P * b:P * b + P], mdf, True))
                    else:
                        hd, bp = b
                        q, r = qbuf[QSLOT[g, f"q{hd // 2}"]], slice(HD * (hd % 2), HD * (hd % 2) + HD)
                        bb = 2 * bp + i
                        lo = P if bb == 0 else 0
                        o = zall[:, base[i] + lo:base[i] + 2 * P]
                        parts.append((slice(P * bb, P * bb + P), slice(P * (bb - 1) + lo, P * (bb + 1)), o, o, mdf if bb == 0 else msw, i == 0))
                    qs, ks, o, m, mask, first = parts[-1]
                    nc.tensor.matmul(o, q[0][r, qs], kk[0][r, ks], start=first, stop=False, skip_group_check=True)
                    nc.tensor.matmul(m, identb, mask, start=False, stop=False, skip_group_check=True)
                    nc.tensor.matmul(o, q[0][r, qs], kk[1][r, ks], start=False, stop=False, skip_group_check=True)
                    mm = nc.tensor.matmul(o, q[1][r, qs], kk[0][r, ks], start=False, stop=True, skip_group_check=True)
                mm.then_inc(z_ready.sem, 1)

            def step_x(L, g, b):
                bank = t_bank(L, ("x", g, b))
                pe.wait_ge(at_ready.sem, at_ready.after(L, ("c", g, b)))
                src = at[steps("s").index(("s", g, b)) % 2]
                n0, n1 = (0, b + 1) if GROUPS[g][0] == "diff" else (1 if b[1] == 0 else 0, 4)
                for j in range(n0, n1):
                    mm = nc.tensor.transpose(bank[:, j * P:(j + 1) * P], src[:, j * P:(j + 1) * P], ident)
                mm.then_inc(t_ready.sem, 1)

            def step_mixn(L, g, i):
                bank = t_bank(L, ("mixn", g, i))
                pe.wait_ge(mix_act.sem, mix_act.after(L, ("mix", g, i)))
                nc.tensor.matmul(bank[:, :], ones, SQ, start=True, stop=True).then_inc(t_ready.sem, 1)

            def out_tile(L, d):
                a = acc[d % 2]
                pe.wait_ge(acc_free.sem, acc_free.nth(L, A_WO + d - 1))
                pe.wait_ge(w_ready.sem, w_ready.nth(L, NT + d + 1))
                slot = (NT + d) % RING
                for k in range(KT):
                    if d == 0:
                        pe.wait_ge(mix_ready.sem, mix_ready.after(L, k))
                    mm = three(a[:, :], (whalf(slot, 0, k), whalf(slot, 1, k)),
                               (mix[0][:, k * SEQ:(k + 1) * SEQ], mix[1][:, k * SEQ:(k + 1) * SEQ]), k == 0, k == KT - 1)
                mm.then_inc(blocks_done.sem, 1)

            def gate_up(L, f, r, first=False):
                for i in range(2):
                    n = f * 2 + i
                    bank = gubank[2 * r + i]
                    if not first:
                        pe.wait_ge(acc_free.sem, acc_free.nth(L, n + (A_GU - 5)))
                    elif r == 0:
                        pe.wait_ge(acc_free.sem, acc_free.nth(L, A_GU - 1 + i))
                    if i == 0 and first and r == 0:
                        pe.wait_ge(h_ready.sem, L * 16 + 16)
                    mm = wblock(L, n + A_GU, (2 * r + i) % RING, bank[:, :], Hs, range(KT), True, True)
                    mm.then_inc(blocks_done.sem, 1)

            def down_tile(L, d, r):
                bank = downbank[r]
                pe.wait_ge(acc_free.sem, acc_free.nth(L, d + (A_DOWN - 2)))
                for half in range(2):
                    n = d * 2 + (N8 + half)
                    slot = (N8 + 2 * r + half) % RING
                    pe.wait_ge(w_ready.sem, w_ready.nth(L, n + 1))
                    for i in range(HALF):
                        k = HALF * half + i
                        if k in (0, FT - 1):
                            pe.wait_ge(ffr.sem, ffr.nth(L, FT - 1 if k == 0 else FT))
                        mm = three(bank[:, :], (whalf(slot, 0, i), whalf(slot, 1, i)),
                                   (ff[0][:, k * SEQ:(k + 1) * SEQ], ff[1][:, k * SEQ:(k + 1) * SEQ]), k == 0, k == FT - 1)
                    mm.then_inc(blocks_done.sem, 1)

            pe.wait_ge(prep, 1)
            nc.tensor.sem_inc(blocks_done.sem, RING)
            with pe.Fori(0, DEPTH) as L:
                z_owner.clear()
                run = {"proj": step_proj, "rstd": rstd_sum, "ms": step_ms, "vt": step_vt, "z": step_z, "cum": step_cum,
                       "pv": step_pv, "s": step_s, "x": step_x, "mixn": step_mixn}
                for s in STEPS:
                    if s[0] in run:
                        run[s[0]](L, *s[1:])
                for d in range(KT):
                    out_tile(L, d)
                for r in range(3):
                    gate_up(L, r, r, first=True)
                    if r == 0:
                        rstd_sum(L, 1)
                with pe.Fori(1, FT // 3) as i:
                    for r in range(3):
                        gate_up(L, i * 3 + r, r)
                gate_up(L, FT - 1, 0)
                with pe.Fori(0, KT // 3) as i:
                    for r in range(3):
                        down_tile(L, i * 3 + r, r)
                for d in range(KT // 3 * 3, KT):
                    down_tile(L, d, d % 3)

        @block.scalar
        def _(act):
            A = nc.scalar.activation
            act.wait_ge(prep, 2)
            A(tables[:, :], tables[:, :], ACT.Sin).then_inc(prep, 1)
            act.wait_ge(prep, 4)
            A(lamw[:, 2 * DEPTH:4 * DEPTH], lamw[:, 0:2 * DEPTH], ACT.Exp).then_inc(prep, 1)

            def x_tile(d, gain, parity, waits):
                xs = X[:, bass.ds(d * SEQ, SEQ)]
                nc.scalar.drain()
                waits()
                A(H[:, bass.ds(d * SEQ, SEQ)], xs, ACT.Copy, scale=gain).then_inc(h_hi.sem, 1)
                A(pbuf[:, parity * SEQ:(parity + 1) * SEQ], xs, ACT.Square).then_inc(x_sq.sem, 1)

            act.wait_ge(loaded, 7 * 16)
            act.wait_ge(xin, KT * 16)
            for k in range(KT):
                def waits(k=k):
                    if k >= 2:
                        act.wait_ge(h_ready.sem, k - 1)
                x_tile(k, gain0[:, k:k + 1], k % 2, waits)

            def norm(L, use, scale, dst, sig):
                act.wait_ge(t_ready.sem, t_ready.after(L, use))
                A(dst, T[T_USES.index(use) % 2][:, :], ACT.Ln, scale=scale, bias=eps).then_inc(t_act.sem, 1)
                nc.scalar.drain()
                A(dst, dst, ACT.Exp, scale=-0.5).then_inc(sig, 1)

            def slot_free(L, g):
                if g >= 2:
                    old = [s for s in steps("z", "cum", "s") if s[1] == g - 2][-1]
                    act.wait_ge(z_ready.sem, z_ready.after(L, old))

            def step_ev(L, t):
                g, role = TILES[t]
                src = pbuf[:, (t % 2) * SEQ:(t % 2 + 1) * SEQ]
                if roped(t):
                    act.wait_ge(acc_free.sem, acc_free.after(L, ("ev", t)))
                    old = before(("ev", t), "ms", "mixn")
                    if old is not None:
                        act.wait_ge(t_ready.sem, t_ready.after(L, old))
                    A(SQ, src, ACT.Square).then_inc(sq_ready.sem, 1)
                elif role != "v":
                    act.wait_ge(acc_free.sem, acc_free.after(L, ("ev", t)))
                    A(qk_buffer(g, role)[0], src, ACT.Copy).then_inc(qk_hi.sem, 1)

            def step_ms(L, t):
                old = before(("ms", t), "ra")
                if old is not None:
                    act.wait_ge(rotated.sem, rotated.after(L, ("rb", old[1])))
                norm(L, ("ms", t), 1.0 / HD, RN, rn_ready.sem)

            def step_rb(L, t):
                g, role = TILES[t]
                slot_free(L, g)
                act.wait_ge(rotated.sem, rotated.after(L, ("rb", t)))
                A(qk_buffer(g, role)[0], Y, ACT.Copy).then_inc(qk_hi.sem, 1)

            def step_vt(L, t):
                g = TILES[t][0]
                use = ("vt", t)
                bank = T[T_USES.index(use) % 2][:, :].rearrange("p (j e) -> p j e", j=NB)
                act.wait_ge(t_ready.sem, t_ready.after(L, use))
                old = [s for s in steps("pv") if s[1] < g]
                if old:
                    assert before(use, "pv") == old[-1]
                    act.wait_ge(pv_done.sem, pv_done.after(L, old[-1]))
                else:
                    act.wait_ge(zeroed.sem, zeroed.after(L, 0))
                if GROUPS[g][0] == "diff":
                    A(vbuf[0][:, :, 0, :], bank, ACT.Copy).then_inc(t_act.sem, 1)
                else:
                    A(vbuf[0][:, :, 0, 0:HD], bank[:, :, 0:HD], ACT.Copy)
                    A(vbuf[0][:, :, 1, HD:P], bank[:, :, HD:P], ACT.Copy)
                    nc.scalar.drain().then_inc(t_act.sem, 1)

            def step_z(L, g, h):
                act.wait_ge(z_ready.sem, z_ready.after(L, ("z", g, h)))
                old = before(("z", g, h), "z")
                if old is not None:
                    act.wait_ge(w_split.sem, w_split.after(L, ("ws",) + old[1:]))
                for b, at0, n in ZE:
                    A(E[:, at0:at0 + n], Z[b][:, 0:n], ACT.Abs)
                nc.scalar.drain()
                A(E, E, ACT.Exp, scale=-1.0)
                nc.scalar.drain()
                A(E, E, ACT.Ln, bias=one).then_inc(ln_ready.sem, 1)

            def step_cum(L, g, h):
                act.wait_ge(z_ready.sem, z_ready.after(L, ("cum", g, h)))
                for b, at0, n in ZE:
                    A(E[:, at0:at0 + n], Z[b][:, 0:n], ACT.Exp)
                nc.scalar.drain().then_inc(w_exp.sem, 1)

            def step_s(L, g, b):
                k = steps("s").index(("s", g, b))
                st = (k % 4) * 8
                z0 = [512 * i for i in banks_of(("s", g, b))]
                act.wait_ge(negmax.sem, negmax.after(L, ("s", g, b)))
                if GROUPS[g][0] == "swa":
                    A(stat[:, st + 6:st + 8], stat[:, st + 2:st + 4], ACT.Exp, bias=cur[:, C_SINK + b[0]:C_SINK + b[0] + 1])
                for i in range(2):
                    lo, hi, e = exp_columns(g, b, i)
                    z = z0[i] if GROUPS[g][0] == "diff" else z0[0]
                    A(e[:, lo:hi], zall[:, z + lo:z + hi], ACT.Exp, bias=stat[:, st + 2 + i:st + 3 + i],
                      accum_out=stat[:, st + 4 + i:st + 5 + i])
                nc.scalar.drain().then_inc(exps.sem, 1)

            def step_x(L, g, b):
                use = ("x", g, b)
                act.wait_ge(t_ready.sem, t_ready.after(L, use))
                act.wait_ge(pv_done.sem, pv_done.after(L, before(use, "pv")))
                bank = T[T_USES.index(use) % 2][:, :].rearrange("p (j e) -> p j e", j=NB)
                for js, q, c0, c1 in pt_parts(use):
                    last = A(pt[0][:, js, q * P:(q + 1) * P], bank[:, c0:c1, :], ACT.Copy)
                if GROUPS[g][0] == "diff":
                    last.then_inc(t_act.sem, 1)
                else:
                    nc.scalar.drain().then_inc(t_act.sem, 1)

            def step_mix(L, g, i):
                m = mix_tile(g, i)
                act.wait_ge(pv_done.sem, pv_done.after(L, ("pv", g, 0 if GROUPS[g][0] == "diff" else 2 * i + 1)))
                if GROUPS[g][0] == "diff":
                    act.wait_ge(t_ready.sem, t_ready.after(L, before(("mix", g, i), "ms")))
                    A(SQ, O[:, :], ACT.Square).then_inc(mix_act.sem, 1)
                else:
                    A(mix[0][:, m * SEQ:(m + 1) * SEQ], O[:, :], ACT.Copy).then_inc(mix_act.sem, 1)

            def step_mixn(L, g, i):
                norm(L, ("mixn", g, i), 1.0 / P, MRN[:, :], mrn_ready.sem)

            def gate_up(L, f, r):
                nc.scalar.drain()
                act.wait_ge(acc_free.sem, acc_free.nth(L, f * 2 + (A_GU + 1)))
                act.wait_ge(loaded, 16)
                A(gbuf[r], gbuf[r], ACT.Silu).then_inc(silu.sem, 1)

            with act.Fori(0, DEPTH) as L:
                norm(L, ("rstd", 0), 1.0 / D_MODEL, rstd[:, :], rstd_ready.sem)
                run = {"ev": step_ev, "ms": step_ms, "rb": step_rb, "vt": step_vt, "z": step_z, "cum": step_cum,
                       "s": step_s, "x": step_x, "mix": step_mix, "mixn": step_mixn}
                for s in STEPS:
                    if s[0] in run:
                        nc.scalar.drain()
                        run[s[0]](L, *s[1:])
                for d in range(KT):
                    def waits(d=d):
                        act.wait_ge(acc_free.sem, acc_free.nth(L, A_WO + d + 1))
                    x_tile(d, cur[:, C_FG + d:C_FG + d + 1], d % 2, waits)
                norm(L, ("rstd", 1), 1.0 / D_MODEL, rstd[:, :], rstd_ready.sem)
                with act.Fori(0, FT // 3) as i:
                    for r in range(3):
                        gate_up(L, i * 3 + r, r)
                gate_up(L, FT - 1, 0)
                with act.Fori(0, KT // 2) as i:
                    for r in range(2):
                        d = i * 2 + r

                        def waits():
                            act.wait_ge(acc_free.sem, acc_free.nth(L, d + (A_DOWN + 1)))
                            act.wait_ge(loaded, 16)
                        x_tile(d, cur[:, bass.ds(d + C_NG, 1)], r, waits)

        @block.vector
        def _(dve):
            V = nc.vector
            drain = V.drain
            tt, ts, stt, cp = V.tensor_tensor, V.tensor_scalar, V.scalar_tensor_tensor, V.tensor_copy

            dve.wait_ge(loaded, 7 * 16)
            cp(constr[:, :], U[:, 0:2 * P])
            cp(constb[:, P:4 * P], U[:, 2 * P:5 * P])
            cp(constb[:, 0:P], ident)
            V.memset(ssum, 0.0)
            drain().then_inc(prep, 1)
            TWO_PI = 2 * np.pi
            C1 = 6.28125
            C2 = float(np.float32(TWO_PI - C1))
            C3 = float(np.float32(TWO_PI - C1 - C2))
            MAGIC = 1.5 * 2.0 ** 23
            PI = 3.1415925
            cp(work[:, 0:SEQ], pbuf[:, 0:SEQ].bitcast(I32))
            drain()
            ts(work[:, 0:SEQ], work[:, 0:SEQ], misc[:, 0:1], None, ALU.mult)
            drain()
            for i, turn in ((0, 0.25), (1, 0.0)):
                n, r = work[:, (1 + i) * SEQ:(2 + i) * SEQ], tables[:, i * SEQ:(i + 1) * SEQ]
                ts(n, work[:, 0:SEQ], 1.0 / TWO_PI, turn, ALU.mult, ALU.add)
                drain()
                ts(n, n, MAGIC, MAGIC, ALU.add, ALU.subtract)
                drain()
                stt(r, n, -C1, work[:, 0:SEQ], ALU.mult, ALU.add)
                drain()
                stt(r, n, -C2, r, ALU.mult, ALU.add)
                drain()
                stt(r, n, -C3, r, ALU.mult, ALU.add)
                drain()
                if i == 0:
                    ts(r, r, np.pi / 2, None, ALU.add)
                    drain()
                ts(r, r, PI, -PI, ALU.min, ALU.max)
            drain().then_inc(prep, 1)
            dve.wait_ge(prep, 3)
            ts(SIN, SIN, misc[:, 1:2], None, ALU.mult)
            for l in range(DEPTH):
                for i in range(2):
                    a = lam[:, (4 * l + 2 * i) * HD:(4 * l + 2 * i + 1) * HD]
                    tt(a, a, lam[:, (4 * l + 2 * i + 1) * HD:(4 * l + 2 * i + 2) * HD], ALU.mult)
                    drain()
                    V.reduce_sum(lamw[:, 2 * l + i:2 * l + i + 1], a, AX_X)
            drain().then_inc(prep, 1)
            dve.wait_ge(prep, 5)
            for l in range(DEPTH):
                o = 2 * DEPTH + 2 * l
                nl = par[:, l * NPAR + C_NLAM:l * NPAR + C_NLAM + 1]
                tt(nl, lamw[:, o + 1:o + 2], lamw[:, o:o + 1], ALU.subtract)
                drain()
                tt(nl, nl, misc[:, 4 + l:5 + l], ALU.subtract)
                g = par[:, l * NPAR + C_SUB:l * NPAR + C_SUB + 1]
                tt(g, g, misc[:, 6 + l:7 + l], ALU.mult)
                for c in (C_DQ, C_WQ):
                    g = par[:, l * NPAR + c:l * NPAR + c + 1]
                    ts(g, g, SCALE, None, ALU.mult)
            drain()

            def x_tile(d, gain, parity):
                xs = X[:, bass.ds(d * SEQ, SEQ)]
                stt(H[:, bass.ds(d * SEQ + KT * SEQ, SEQ)], xs, gain, H[:, bass.ds(d * SEQ, SEQ)].bitcast(F32),
                    ALU.mult, ALU.subtract).then_inc(h_ready.sem, 1)

            def square_sum(parity):
                return tt(ssum, ssum, pbuf[:, parity * SEQ:(parity + 1) * SEQ], ALU.add)

            for k in range(KT):
                drain()
                dve.wait_ge(x_sq.sem, k + 1)
                square_sum(k % 2)
                x_tile(k, gain0[:, k:k + 1], k % 2)
            drain().then_inc(ssum_ready.sem, 1)

            def step_ev(L, t):
                g, role = TILES[t]
                if t == 0:
                    dve.wait_ge(rstd_ready.sem, rstd_ready.after(L, ("rstd", 0)))
                dve.wait_ge(blocks_done.sem, blocks_done.nth(L, t + 1))
                c = SCALE if role == "q0" and GROUPS[g][0] == "sb" else 1.0
                stt(pbuf[:, (t % 2) * SEQ:(t % 2 + 1) * SEQ], acc[t % 2][:, :], c, rstd[:, :], ALU.mult, ALU.mult)\
                    .then_inc(acc_free.sem, 1)
                if t == 1:
                    V.memset(vbuf[0].bitcast(F32), 0.0)
                    V.memset(vbuf[1].bitcast(F32), 0.0)
                    drain().then_inc(zeroed.sem, 1)

            def step_ra(L, t):
                g, role = TILES[t]
                gain = {"diff": {"q0": C_DQ, "k": C_DK}, "swa": {"q0": C_WQ, "q1": C_WQ, "k": C_WK}}[GROUPS[g][0]][role]
                old = before(("ra", t), "rl")
                if old is not None and roped(old[1]):
                    dve.wait_ge(qk_hi.sem, qk_hi.after(L, old))
                dve.wait_ge(rn_ready.sem, rn_ready.after(L, ("ms", t)))
                stt(Y, pbuf[:, (t % 2) * SEQ:(t % 2 + 1) * SEQ], cur[:, gain:gain + 1], RN, ALU.mult, ALU.mult)
                drain()
                V.stream_shuffle(ROT, Y, [(i + 16) % 32 for i in range(32)])
                tt(Y, Y, COS, ALU.mult)

            def step_rb(L, t):
                tt(ROT, ROT, SIN, ALU.mult)
                drain()
                tt(Y, Y, ROT, ALU.add).then_inc(rotated.sem, 1)

            def step_rl(L, t):
                g, role = TILES[t]
                hi, lo = qk_buffer(g, role)
                src = Y if roped(t) else pbuf[:, (t % 2) * SEQ:(t % 2 + 1) * SEQ]
                dve.wait_ge(qk_hi.sem, qk_hi.after(L, ("rl", t)))
                tt(lo, src, hi.bitcast(F32), ALU.subtract).then_inc(qk_ready.sem, 1)

            def step_vl(L, t):
                bank = T[T_USES.index(("vt", t)) % 2][:, :].rearrange("p (j e) -> p j e", j=NB)
                dve.wait_ge(t_act.sem, t_act.after(L, ("vt", t)))
                hi, lo = vbuf
                if GROUPS[TILES[t][0]][0] == "diff":
                    tt(lo[:, :, 0, :], bank, hi[:, :, 0, :].bitcast(F32), ALU.subtract).then_inc(t_dve.sem, 1)
                else:
                    tt(lo[:, :, 0, 0:HD], bank[:, :, 0:HD], hi[:, :, 0, 0:HD].bitcast(F32), ALU.subtract)
                    tt(lo[:, :, 1, HD:P], bank[:, :, HD:P], hi[:, :, 1, HD:P].bitcast(F32), ALU.subtract)
                    drain().then_inc(t_dve.sem, 1)

            def step_sp(L, g, h):
                dve.wait_ge(ln_ready.sem, ln_ready.after(L, ("z", g, h)))
                for b, at0, n in ZE:
                    stt(E[:, at0:at0 + n], Z[b][:, 0:n], 0.0, E[:, at0:at0 + n], ALU.max, ALU.add)
                drain()
                cp(spb[0], E)
                drain()
                tt(spb[1], E, spb[0].bitcast(F32), ALU.subtract).then_inc(sp_ready.sem, 1)

            def step_ws(L, g, h):
                dve.wait_ge(w_exp.sem, w_exp.after(L, ("cum", g, h)))
                old = before(("ws", g, h), "pv")
                if old is not None:
                    dve.wait_ge(pv_done.sem, pv_done.after(L, old))
                for j in range(NB):
                    cp(pt[0][:, j, P * j:SEQ], epart(E, j))
                drain()
                for j in range(NB):
                    tt(pt[1][:, j, P * j:SEQ], epart(E, j), pt[0][:, j, P * j:SEQ].bitcast(F32), ALU.subtract)
                drain().then_inc(w_split.sem, 1)

            def step_s(L, g, b):
                st = (steps("s").index(("s", g, b)) % 4) * 8
                used = banks_of(("s", g, b))
                at0 = 512 * used[0]
                dve.wait_ge(z_ready.sem, z_ready.after(L, ("s", g, b)))
                if GROUPS[g][0] == "diff":
                    z = zall[:, :].rearrange("p (c k) -> p c k", c=3)[:, used[0]:used[1] + 1:used[1] - used[0], 0:P * (b + 1)]
                    V.reduce_max(stat[:, st:st + 2], z, AX_X)
                    drain()
                    ts(stat[:, st + 2:st + 4], stat[:, st:st + 2], -1.0, None, ALU.mult).then_inc(negmax.sem, 1)
                else:
                    hd, bp = b
                    if bp == 0:
                        V.reduce_max(stat[:, st:st + 1], zall[:, at0 + P:at0 + 2 * P], AX_X)
                        V.reduce_max(stat[:, st + 1:st + 2], zall[:, at0 + 2 * P:at0 + 4 * P], AX_X)
                    else:
                        V.reduce_max(stat[:, st:st + 2], zall[:, at0:at0 + 4 * P].rearrange("p (b k) -> p b k", b=2), AX_X)
                    drain()
                    ts(stat[:, st + 2:st + 4], stat[:, st:st + 2], cur[:, C_SINK + hd:C_SINK + hd + 1], -1.0,
                       ALU.max, ALU.mult).then_inc(negmax.sem, 1)

            def step_c(L, g, b):
                k = steps("s").index(("s", g, b))
                st = (k % 4) * 8
                dve.wait_ge(exps.sem, exps.after(L, ("s", g, b)))
                if k >= 2:
                    old = steps("s")[k - 2]
                    dve.wait_ge(t_ready.sem, t_ready.after(L, ("x",) + old[1:]))
                dst = at[k % 2]
                (lo0, hi0, e0), (lo1, hi1, e1) = exp_columns(g, b, 0), exp_columns(g, b, 1)
                if GROUPS[g][0] == "diff":
                    V.reciprocal(stat[:, st + 6:st + 8], stat[:, st + 4:st + 6])
                    drain()
                    ts(e1[:, 0:hi1], e1[:, 0:hi1], stat[:, st + 7:st + 8], cur[:, C_NLAM:C_NLAM + 1], ALU.mult, ALU.mult)
                    drain()
                    stt(dst[:, 0:hi0], e0[:, 0:hi0], stat[:, st + 6:st + 7], e1[:, 0:hi0], ALU.mult, ALU.add).then_inc(at_ready.sem, 1)
                else:
                    tt(stat[:, st + 4:st + 6], stat[:, st + 4:st + 6], stat[:, st + 6:st + 8], ALU.add)
                    drain()
                    V.reciprocal(stat[:, st + 6:st + 8], stat[:, st + 4:st + 6])
                    drain()
                    ts(dst[:, lo0:hi0], e0[:, lo0:hi0], stat[:, st + 6:st + 7], None, ALU.mult)
                    ts(dst[:, lo1:hi1], e1[:, lo1:hi1], stat[:, st + 7:st + 8], None, ALU.mult)
                    drain().then_inc(at_ready.sem, 1)

            def step_xl(L, g, b):
                use = ("x", g, b)
                dve.wait_ge(t_act.sem, t_act.after(L, use))
                bank = T[T_USES.index(use) % 2][:, :].rearrange("p (j e) -> p j e", j=NB)
                for js, q, c0, c1 in pt_parts(use):
                    last = tt(pt[1][:, js, q * P:(q + 1) * P], bank[:, c0:c1, :], pt[0][:, js, q * P:(q + 1) * P].bitcast(F32), ALU.subtract)
                if GROUPS[g][0] == "diff":
                    last.then_inc(t_dve.sem, 1)
                else:
                    drain().then_inc(t_dve.sem, 1)

            def step_mixl(L, g, i):
                m = mix_tile(g, i)
                hi, lo = (mix[part][:, m * SEQ:(m + 1) * SEQ] for part in range(2))
                if GROUPS[g][0] == "diff":
                    dve.wait_ge(mrn_ready.sem, mrn_ready.after(L, ("mixn", g, i)))
                    stt(MRN[:, :], O[:, :], cur[:, C_SUB:C_SUB + 1], MRN[:, :], ALU.mult, ALU.mult)
                    drain()
                    cp(hi, MRN[:, :])
                    drain()
                    tt(lo, MRN[:, :], hi.bitcast(F32), ALU.subtract).then_inc(mix_ready.sem, 1)
                else:
                    dve.wait_ge(mix_act.sem, mix_act.after(L, ("mix", g, i)))
                    tt(lo, O[:, :], hi.bitcast(F32), ALU.subtract).then_inc(mix_ready.sem, 1)

            def gate_up(L, f, r):
                g, u = gubank[2 * r], gubank[2 * r + 1]
                drain()
                dve.wait_ge(rstd_ready.sem, rstd_ready.after(L, ("rstd", 1)))
                dve.wait_ge(blocks_done.sem, blocks_done.nth(L, f * 2 + (A_GU + 1)))
                tt(gbuf[r], g[:, :], rstd[:, :], ALU.mult).then_inc(acc_free.sem, 1)
                dve.wait_ge(blocks_done.sem, blocks_done.nth(L, f * 2 + (A_GU + 2)))
                tt(ubuf[r], u[:, :], rstd[:, :], ALU.mult).then_inc(acc_free.sem, 1)
                drain()
                dve.wait_ge(silu.sem, silu.nth(L, f + 1))
                tt(ubuf[r], ubuf[r], gbuf[r], ALU.mult)
                drain()
                cp(ff[0][:, bass.ds(f * SEQ, SEQ)], ubuf[r])
                drain()
                tt(ff[1][:, bass.ds(f * SEQ, SEQ)], ubuf[r], ff[0][:, bass.ds(f * SEQ, SEQ)].bitcast(F32), ALU.subtract)\
                    .then_inc(ffr.sem, 1)

            def x_stage_tile(L, blocks, n0, d, bank, gain, r):
                xs = X[:, bass.ds(d * SEQ, SEQ)]
                drain()
                dve.wait_ge(blocks_done.sem, blocks_done.nth(L, blocks))
                tt(xs, xs, bank[:, :], ALU.add).then_inc(acc_free.sem, 1)
                drain()
                dve.wait_ge(x_sq.sem, x_sq.nth(L, d + (n0 + 1)))
                square_sum(r)
                x_tile(d, gain, r)

            with dve.Fori(0, DEPTH) as L:
                cp(cur[:, :], par[:, bass.ds(L * NPAR, NPAR)])
                drain()
                run = {"ev": step_ev, "ra": step_ra, "rb": step_rb, "rl": step_rl, "vl": step_vl, "sp": step_sp,
                       "ws": step_ws, "s": step_s, "c": step_c, "xl": step_xl, "mixl": step_mixl}
                for s in STEPS:
                    if s[0] in run:
                        drain()
                        run[s[0]](L, *s[1:])
                V.memset(ssum, 0.0)
                drain()
                for d in range(KT):
                    x_stage_tile(L, NT + d + 1, 0, d, acc[d % 2], cur[:, C_FG + d:C_FG + d + 1], d % 2)
                drain().then_inc(ssum_ready.sem, 1)
                with dve.Fori(0, FT // 3) as i:
                    for r in range(3):
                        gate_up(L, i * 3 + r, r)
                gate_up(L, FT - 1, 0)
                V.memset(ssum, 0.0)
                drain()
                for d in range(KT):
                    x_stage_tile(L, N8 + 2 * d + 2, KT, d, downbank[d % 3], cur[:, C_NG + d:C_NG + d + 1], d % 2)
                drain().then_inc(ssum_ready.sem, 1)


def _launch_layout(inputs):
    f32 = np.float32
    g = {k: np.asarray(v) for k, v in inputs.items()}
    perm = np.concatenate([np.arange(0, 16), np.arange(32, 48), np.arange(16, 32), np.arange(48, 64)])
    perm2 = np.concatenate([perm, HD + perm])
    sbw, dqk, dw = 256, 512, 512
    o_sq, o_sk, o_sv = 0, sbw, 2 * sbw
    o_dq, o_dk, o_dv = 3 * sbw, 3 * sbw + dqk, 3 * sbw + 2 * dqk
    o_wq = o_dv + dw
    o_wk, o_wv = o_wq + 256, o_wq + 256 + 128
    cols = []
    for (grp, role) in TILES:
        kind, i = GROUPS[grp]
        if kind == "sb":
            cols.append({"q0": o_sq, "k": o_sk, "v": o_sv}[role] + i * P + np.arange(P))
        elif kind == "diff":
            cols.append({"q0": o_dq, "k": o_dk, "v": o_dv}[role] + i * P + (np.arange(P) if role == "v" else perm2))
        elif role[0] == "q":
            t = int(role[1])
            cols.append(o_wq + np.concatenate([t * HD + perm, (t + 2) * HD + perm]))
        else:
            cols.append({"k": o_wk + perm2, "v": o_wv + np.arange(P)}[role])
    cols = np.concatenate(cols)
    c0 = sbw + dw
    rows = np.concatenate([np.arange(sbw)] + [c0 + h * HD + np.arange(HD) for h in (0, 2, 1, 3)] + [sbw + np.arange(dw)])

    def blocks(w):
        return w.reshape(w.shape[0] // P, P, w.shape[1] // P, P).transpose(2, 1, 0, 3)
    w8, w11 = [], []
    for l in range(DEPTH):
        w8.append(blocks(g["w_in"][l][:, cols]))
        w8.append(blocks(g["w_o"][l][rows]))
        gu = np.stack([blocks(g["w_gate"][l]), blocks(g["w_up"][l])], axis=1)
        w8.append(gu.reshape(2 * FT, P, KT, P))
        w11.append(blocks(g["w_down"][l]).reshape(KT, P, 2, HALF, P).transpose(0, 2, 1, 3, 4).reshape(N11, P, HALF, P))
    w8 = np.concatenate(w8).reshape(DEPTH * N8, P, KT * P)
    w11 = np.concatenate(w11).reshape(DEPTH * N11, P, HALF * P)
    par = [g["attn_norm_g"][0].reshape(KT, P).T]
    for l in range(DEPTH):
        two = lambda v: np.concatenate([v[l][perm], v[l][perm]])[:, None]
        nxt = g["attn_norm_g"][(l + 1) % DEPTH]
        par += [g["ffn_norm_g"][l].reshape(KT, P).T, nxt.reshape(KT, P).T,
                two(g["diff_q_norm_g"]), two(g["diff_k_norm_g"]), two(g["swa_q_norm_g"]), two(g["swa_k_norm_g"]),
                g["diff_subln_g"][l][:, None],
                np.tile(g["swa_sinks"][l][[0, 2, 1, 3]][None, :], (P, 1)), np.zeros((P, 1), f32)]
    par = np.concatenate(par, axis=1)
    lam = np.tile(g["diff_lambda"].reshape(1, -1), (P, 1))
    misc = np.zeros((P, 8), f32)
    inv = f32(1) / f32(ROPE_THETA) ** (np.arange(0, HD, 2, dtype=f32) / f32(HD))
    misc[:, 0] = inv[perm2 % HD % 32]
    misc[:, 1] = np.where(perm2 % HD < 32, -1.0, 1.0)
    misc[:, 2] = EPS
    misc[:, 3] = 1.0
    for l in range(DEPTH):
        li = 0.8 - 0.6 * np.exp(-0.3 * l)
        misc[:, 4 + l], misc[:, 6 + l] = li, 1.0 - li
    i, j = np.arange(P)[:, None], np.arange(P)[None, :]
    const = np.zeros((P, NCONST), f32)
    const[:, K_ID:K_ID + P] = i == j
    const[:, K_BLK:K_BLK + P] = i // HD == j // HD
    const[:, K_ONE:K_ONE + P] = 1.0
    const[:, K_TRI:K_TRI + P] = -1.0 * (i >= j)
    const[:, K_NEG1:K_NEG1 + P] = -1.0
    const[:, K_MSB:K_MSB + P] = NEG * (i >= j)
    const[:, K_MSW:K_MSW + P] = NEG * ((j < CHUNK) | (i >= CHUNK))
    const[:, K_MDF:K_MDF + P] = NEG * ((i < CHUNK) & (j >= CHUNK))
    x = g["x"].reshape(SEQ, KT, P).transpose(1, 2, 0)
    pos = np.tile(g["positions"].reshape(1, SEQ), (P, 1))
    return [("x", x), ("pos", pos), ("w8", w8), ("w11", w11), ("par", par), ("lam", lam), ("misc", misc), ("const", const)]


def kernel(**inputs):
    import concourse.bacc as _bacc
    from concourse.bass_utils import run_bass_kernel_spmd as _run

    nc = _bacc.Bacc("TRN2", target_bir_lowering=False, num_devices=1, dynamic_dma_scratch_size=1024)
    arrays, args = {}, []
    for name, a in _launch_layout(inputs):
        a = np.ascontiguousarray(a)
        arrays[f"in_{name}"] = a
        args.append(nc.dram_tensor(f"in_{name}", a.shape, mybir.dt.from_np(a.dtype), kind="ExternalInput").ap())
    out = nc.dram_tensor("out_x", (KT, P, SEQ), F32, kind="ExternalOutput").ap()
    trunk_kernel(nc, *args, out)
    r = _run(nc, [arrays], core_ids=[0])
    y = r.results[0]["out_x"]
    return np.ascontiguousarray(y.transpose(2, 0, 1).reshape(1, SEQ, D_MODEL))
```

```python
from contextlib import ExitStack

import concourse.bass as bass
import numpy as np
from concourse import mybir

F32 = mybir.dt.float32
F32R = mybir.dt.float32r
BF16 = mybir.dt.bfloat16
I32 = mybir.dt.int32
ACT = mybir.ActivationFunctionType
ALU = mybir.AluOpType
AX_X = mybir.AxisListType.X

P = 128
D_MODEL = 1024
SEQ = 512
DEPTH = 2
HD = 64
CHUNK = 64
ROPE_THETA = 10000.0
EPS = 1e-6
D_FF = -(-8 * D_MODEL // (3 * 256)) * 256
SCALE = HD ** -0.5
KT = D_MODEL // P
FT = D_FF // P
NB = SEQ // P
NEG = -1e30

GROUPS = [("sb", 0), ("sb", 1), ("swa", 0), ("diff", 0), ("diff", 1), ("diff", 2), ("diff", 3)]
TILES = []
for _g, (_kind, _i) in enumerate(GROUPS):
    for _role in (["q0", "q1", "k", "v"] if _kind == "swa" else ["q0", "k", "v"]):
        TILES.append((_g, _role))
NT = len(TILES)
QSLOT = {(0, "q0"): 0, (1, "q0"): 1, (2, "q0"): 0, (2, "q1"): 2, (3, "q0"): 1, (4, "q0"): 0, (5, "q0"): 1, (6, "q0"): 0}

HALF = FT // 2
N8 = NT + KT + 2 * FT
N11 = 2 * KT
WPER = N8 + N11
RING = 3
assert WPER % RING == 0 and (NT + KT) % RING == 0
A_WO, A_GU, A_DOWN = NT, NT + KT, NT + KT + 2 * FT
ACCS = A_DOWN + KT

C_FG, C_NG, C_DQ, C_DK, C_WQ, C_WK, C_SUB, C_SINK, C_NLAM, NPAR = 0, 8, 16, 17, 18, 19, 20, 21, 25, 26
K_ID, K_BLK, K_ONE, K_TRI, K_NEG1, K_MSB, K_MSW, K_MDF, NCONST = (P * i for i in range(9))


PROJ_PARTS = 4


class Signal:

    def __init__(self, sem, events, before=0):
        self.sem, self.before = sem, before
        self.count = {e: i + 1 for i, e in enumerate(events)}
        self.per = len(events)

    def after(self, L, event):
        return L * self.per + (self.before + self.count[event])

    def nth(self, L, n):
        return L * self.per + (n + self.before)


TILE_LAGS = {"ev": 4, "ms": 6, "ra": 7, "rb": 8, "rl": 9, "plain_rl": 5, "vt": 11, "vl": 11}
SB_SLOTS = [11, 19, 27, 35]
SB_LAGS = [-1, 2, 5, 5, 11]
SB_MIX = 2
SW_SLOTS = [45, 49, 52, 54]
SW_LAGS = {"s": 0, "c": 0, "x": 3, "xl": 3, "pv": 5, "mix": 5}
DF_SLOTS = [58, 70, 82, 94]
DF_BLOCKS = [-2, 0, 2, 3]
DF_LAGS = {"s": 0, "c": 0, "x": 4, "xl": 4, "pv": 12, "mix": 14, "mixn": 14, "mixl": 22}
WO_SLOTS = {(0, 0): 88, (1, 0): 93, (0, 1): 99, (1, 1): 108, (2, 0): 100, (2, 1): 101, (0, 2): 119, (1, 2): 132, (2, 2): 121}
WITHIN = ["mix", "ra", "s", "mixn", "vl", "ms", "pv", "vt", "rstd", "cum", "x"]
WITHIN += ["ev", "rb", "mixl", "sp", "z", "rl", "ws", "proj", "c", "xl", "wo"]


def attention_steps():
    placed = []

    def place(slot, *step):
        placed.append((slot, WITHIN.index(step[0]), len(placed), step))

    place(PROJ_PARTS, "rstd", 0)
    for t, (g, role) in enumerate(TILES):
        for part in range(PROJ_PARTS):
            place(PROJ_PARTS * t + part, "proj", t, part)
        place(PROJ_PARTS * t + TILE_LAGS["ev"], "ev", t)
        if role == "v":
            kinds = ("vt", "vl")
        elif roped(t):
            kinds = ("ms", "ra", "rb", "rl")
        else:
            kinds = ("plain_rl",)
        for kind in kinds:
            place(PROJ_PARTS * t + TILE_LAGS[kind], kind.removeprefix("plain_"), t)
    for n, a in enumerate(SB_SLOTS):
        g, h = divmod(n, 2)
        for kind, i in zip(("z", "sp", "cum", "ws", "pv"), SB_LAGS):
            place(a + i, kind, g, h)
        if h:
            place(a + SB_LAGS[4] + SB_MIX, "mix", g, 0)
            place(a + SB_LAGS[4] + SB_MIX, "mixl", g, 0)
    for hd, a in enumerate(SW_SLOTS):
        for half in range(2):
            for kind in ("s", "c", "x", "xl"):
                place(a + SW_LAGS[kind], kind, 2, (hd, half))
        place(a + SW_LAGS["pv"], "pv", 2, hd)
        if hd % 2:
            place(a + SW_LAGS["mix"], "mix", 2, hd // 2)
            place(a + SW_LAGS["mix"], "mixl", 2, hd // 2)
    for g, a in zip(range(3, 7), DF_SLOTS):
        for b in range(NB):
            for kind in ("s", "c", "x", "xl"):
                place(a + DF_BLOCKS[b] + DF_LAGS[kind], kind, g, b)
        for kind in ("pv", "mix", "mixn", "mixl"):
            place(a + DF_LAGS[kind], kind, g, 0)
    for (d, part), a in WO_SLOTS.items():
        place(a, "wo", d, part)
    return [p[3] for p in sorted(placed)]


def roped(t):
    return GROUPS[TILES[t][0]][0] != "sb" and TILES[t][1] != "v"


STEPS = attention_steps()
WO_PARTS = [range(0, 4), range(4, 6), range(6, 7), range(7, 8)]
T_USES = [s for s in STEPS if s[0] in ("rstd", "x", "mixn", "ms", "vt")] + [("rstd", 1)]
LO_OF = {"x": "xl", "vt": "vl"}


def steps(*kinds):
    return [s for s in STEPS if s[0] in kinds]


def before(step, *kinds):
    found = [s for s in STEPS[:STEPS.index(step)] if s[0] in kinds]
    return found[-1] if found else None


def mix_tile(g, i):
    return {"sb": g, "swa": 2 + i, "diff": g + 1}[GROUPS[g][0]]


def banks_of(step):
    if step[0] == "z":
        return [0, 1, 2]
    k = steps("s").index(step) % 3
    return [k] if GROUPS[step[1]][0] == "swa" else [[0, 1], [0, 2], [1, 2]][k]


def trunk_kernel(nc, x_in, pos_in, w8_in, w11_in, par_in, lam_in, misc_in, const_in, out):
    ctx = ExitStack()
    with ctx:
        def sb(name, cols, dt=F32):
            return ctx.enter_context(nc.sbuf_tensor(name, [P, cols], dt))

        def sem(name):
            return ctx.enter_context(nc.semaphore(name))

        X = sb("X", KT * SEQ)
        H = sb("H", 2 * KT * SEQ, F32R)
        raw = sb("raw", RING * HALF * P)
        W = sb("W", RING * 2 * HALF * P, F32R)
        R = sb("R", 2 * FT * SEQ, F32R)
        tables = sb("tables", 2 * SEQ)
        pbuf = sb("pbuf", 2 * SEQ)
        work = sb("work", 4 * SEQ)
        MRN = sb("MRN", SEQ)
        U = sb("U", 6 * SEQ)
        rstd = sb("rstd", SEQ)
        par = sb("par", DEPTH * NPAR)
        gain0 = sb("gain0", KT)
        cur = sb("cur", NPAR)
        lamw = sb("lamw", 8 * DEPTH)
        misc = sb("misc", 8)
        const = sb("const", 3 * P)
        constr = sb("constr", 2 * P, F32R)
        constb = sb("constb", 4 * P, BF16)
        stat = sb("stat", 32)
        idle = sb("idle", 2)

        def rpart(at, n):
            return R[:, at * SEQ:(at + n) * SEQ]
        mix = [rpart(0, KT), rpart(KT, KT)]
        qbuf = [[rpart(16 + 2 * s, 1), rpart(17 + 2 * s, 1)] for s in range(2)] + [[rpart(41, 1), rpart(42, 1)]]
        kbuf = [[rpart(20 + 2 * s, 1), rpart(21 + 2 * s, 1)] for s in range(2)]
        vbuf = [rpart(24 + 2 * s, 2).rearrange("p (j a e) -> p j a e", j=NB, a=2) for s in range(2)]
        pt = [rpart(28 + 4 * s, 4).rearrange("p (j q) -> p j q", j=NB) for s in range(2)]
        spb = [R[:, 36 * SEQ:36 * SEQ + 1280], R[:, 36 * SEQ + 1280:36 * SEQ + 2560]]
        ff = [rpart(0, FT), rpart(FT, FT)]
        lam = U[:, 2 * SEQ:2 * SEQ + DEPTH * 4 * HD]
        pos = U[:, 4 * SEQ:5 * SEQ]
        sqbuf = [pbuf[:, 0:SEQ], pbuf[:, SEQ:2 * SEQ], MRN[:, :]]
        SQ, RN, Y, ROT = (work[:, i * SEQ:(i + 1) * SEQ] for i in range(4))
        ssum = ROT
        COS, SIN = tables[:, 0:SEQ], tables[:, SEQ:2 * SEQ]
        E = U[:, 0:1280]
        eb = [U[:, i * SEQ:(i + 1) * SEQ] for i in range(4)]
        at = [U[:, (4 + i) * SEQ:(5 + i) * SEQ] for i in range(2)]
        gbuf = [U[:, i * SEQ:(i + 1) * SEQ] for i in range(3)]
        ubuf = [U[:, (3 + i) * SEQ:(4 + i) * SEQ] for i in range(3)]
        ident, blk, ones = (const[:, i * P:(i + 1) * P] for i in range(3))
        tri, neg1 = constr[:, 0:P], constr[:, P:2 * P]
        identb, msb = constb[:, 0:P], constb[:, P:2 * P]
        msw, mdf = constb[:, 2 * P:4 * P], constb[:, 3 * P:4 * P]
        eps, one = misc[:, 2:3], misc[:, 3:4]

        banks = [ctx.enter_context(nc.psum_tensor(f"bank{i}", [P, 512], F32)) for i in range(2)]
        zall = ctx.enter_context(nc.psum_tensor("scores", [P, 3 * 512], F32))
        Z = [zall[:, 512 * i:512 * (i + 1)] for i in range(3)]
        banks += Z + [ctx.enter_context(nc.psum_tensor(f"bank{i}", [P, 512], F32)) for i in range(5, 8)]
        acc, O, T = banks[0:2], banks[5], banks[6:8]
        gubank = banks[0:6]
        wobank = banks[0:3]
        downbank = banks[2:5]
        zreg = [(0, 0, 512), (1, 0, 384), (2, 0, 256), (1, 384, 128)]
        eoff = [0, 512, 1024, 896]

        def zpart(j, skip=0):
            b, c, n = zreg[j]
            return Z[b][:, c + skip:c + n]

        def epart(buf, j):
            return buf[:, eoff[j]:eoff[j] + SEQ - P * j]
        ZE = [(0, 0, 512), (1, 512, 512), (2, 1024, 256)]

        loaded, gained, angles = sem("loaded"), sem("gain_loaded"), sem("positions_loaded")
        xin = [sem(f"x_loaded{k}") for k in range(KT)]
        prep = sem("prepared")
        raw_ready = [sem(f"raw_ready{s}") for s in range(RING)]
        first_hi = sem("first_blocks_hi")
        out_done = sem("out_done")
        tiles8 = [("wo", d) for d in range(KT)] + [("down", d) for d in range(KT)]
        acc_names = [("ev", t) for t in range(NT)] + [("wo", d) for d in range(KT)] + [(r, f) for f in range(FT) for r in "gu"] + [("down", d) for d in range(KT)]
        w_hi = Signal(sem("w_hi_ready"), range(RING, WPER))
        w_ready = Signal(sem("w_ready"), range(WPER), before=RING)
        blocks_done = Signal(sem("blocks_done"), range(WPER), before=RING)
        acc_free = Signal(sem("acc_free"), acc_names)
        t_ready = Signal(sem("t_ready"), T_USES)
        t_act = Signal(sem("t_read_act"), T_USES)
        t_dve = Signal(sem("t_read_dve"), steps(*LO_OF.values()))
        z_ready = Signal(sem("z_ready"), steps("z", "cum", "s"))
        pv_done = Signal(sem("pv_done"), steps("pv"))
        ln_ready = Signal(sem("ln_ready"), steps("z"))
        sp_ready = Signal(sem("softplus_ready"), steps("sp"))
        w_exp = Signal(sem("weights_exp"), steps("cum"))
        w_split = Signal(sem("weights_split"), steps("ws"))
        negmax = Signal(sem("negmax_ready"), steps("s"))
        exps = Signal(sem("exp_ready"), steps("s"))
        at_ready = Signal(sem("probs_ready"), steps("c"))
        sq_ready = Signal(sem("squares_ready"), [s for s in steps("ev") if roped(s[1])])
        rn_ready = Signal(sem("headnorm_ready"), steps("ms"))
        rotated = Signal(sem("rotated"), steps("rb"))
        qk_hi = Signal(sem("qk_hi_ready"), [("rl", s[1]) for s in STEPS if s[0] == "rb" or (s[0] == "ev" and not roped(s[1]) and TILES[s[1]][1] != "v")])
        qk_ready = Signal(sem("qk_ready"), steps("rl"))
        mix_act = Signal(sem("mix_act"), steps("mix"))
        mrn_ready = Signal(sem("mixnorm_ready"), steps("mixn"))
        mix_ready = Signal(sem("mix_ready"), range(KT))
        h_hi = Signal(sem("h_hi_ready"), tiles8, before=KT)
        x_sq = Signal(sem("x_squares"), tiles8, before=KT)
        h_ready = Signal(sem("h_ready"), tiles8, before=KT)
        ssum_ready = Signal(sem("ssum_ready"), ["wo", "down"], before=1)
        rstd_ready = Signal(sem("rstd_ready"), [("rstd", 0), ("rstd", 1)])
        silu = Signal(sem("silu_ready"), range(FT))
        zeroed = Signal(sem("values_zeroed"), [0])
        ffr = Signal(sem("ff_ready"), range(FT))

        block = ctx.enter_context(nc.Block())

        def pt_parts(step):
            _, g, b = step
            if GROUPS[g][0] == "diff":
                return [(slice(0, b + 1), b, 0, b + 1)]
            out_ = []
            for i in range(2):
                bb = 2 * b[1] + i
                j0 = max(bb - 1, 0)
                out_.append((slice(j0, bb + 1), bb, 2 * i + (1 if bb == 0 else 0), 2 * i + 2))
            return out_

        def exp_columns(g, b, i):
            k = 2 * (steps("s").index(("s", g, b)) % 2)
            if GROUPS[g][0] == "diff":
                return 0, P * (b + 1), eb[k + i]
            return 2 * P * i + (P if b[1] == i == 0 else 0), 2 * P * (i + 1), eb[k]

        def qk_buffer(g, role):
            return kbuf[g % 2] if role == "k" else qbuf[QSLOT[g, role]]

        @block.sync
        def _(sp):
            def load(L, n, src, cols, slot):
                sp.wait_ge(w_ready.sem, L * WPER + (n + 1))
                sp.dma_start(raw[:, slot * HALF * P:slot * HALF * P + cols], src).then_inc(raw_ready[slot], 16)

            with sp.Fori(0, DEPTH) as L:
                with sp.Fori(0, N8 // RING) as i:
                    for s in range(RING):
                        load(L, i * RING + s, w8_in[bass.ds(L * N8 + i * RING + s, 1)].rearrange("o p c -> p (o c)"), KT * P, s)
                for n in range(N8 // RING * RING, N8):
                    load(L, n, w8_in[bass.ds(L * N8 + n, 1)].rearrange("o p c -> p (o c)"), KT * P, n % RING)
                load(L, N8, w11_in[bass.ds(L * N11, 1)].rearrange("o p c -> p (o c)"), HALF * P, N8 % RING)
                with sp.Fori(0, (N11 - 1) // RING) as i:
                    for s in range(RING):
                        n = i * RING + s + 1
                        load(L, n + N8, w11_in[bass.ds(L * N11 + n, 1)].rearrange("o p c -> p (o c)"), HALF * P, (N8 + 1 + s) % RING)
            for d in range(KT):
                sp.wait_ge(acc_free.sem, acc_free.after(DEPTH - 1, ("down", d)))
                sp.dma_start(out[d], X[:, d * SEQ:(d + 1) * SEQ]).then_inc(out_done, 16)
            sp.wait_ge(out_done, 16 * KT)

        @block.gpsimd
        def _(pool):
            nc.gpsimd.memset(idle[:, 0:1], 0.0).then_inc(w_ready.sem, RING)
            pool.wait_ge(w_ready.sem, RING)

            def parts(cols, slot):
                return (raw[:, slot * HALF * P:slot * HALF * P + cols],
                        W[:, 2 * slot * HALF * P:2 * slot * HALF * P + cols],
                        W[:, (2 * slot + 1) * HALF * P:(2 * slot + 1) * HALF * P + cols])

            def first_block(L, n):
                src, hi, lo = parts(KT * P, n)
                pool.wait_ge(blocks_done.sem, L * WPER + (n + 1))
                pool.wait_ge(raw_ready[n], L * (16 * WPER // RING) + 16)
                nc.gpsimd.tensor_tensor(idle[:, 1:2], idle[:, 0:1], idle[:, 0:1], ALU.mult)
                nc.gpsimd.tensor_scalar(hi, src, 1.0, None, ALU.mult).then_inc(first_hi, 1)
                pool.wait_ge(first_hi, L * RING + (n + 1))
                nc.gpsimd.tensor_tensor(lo, src, hi.bitcast(F32), ALU.subtract).then_inc(w_ready.sem, 1)

            def split_lo(L, n, cols, slot):
                src, hi, lo = parts(cols, slot)
                pool.wait_ge(w_hi.sem, w_hi.nth(L, n + (1 - RING)))
                nc.gpsimd.tensor_tensor(lo, src, hi.bitcast(F32), ALU.subtract).then_inc(w_ready.sem, 1)

            with pool.Fori(0, DEPTH) as L:
                for n in range(RING):
                    first_block(L, n)
                with pool.Fori(1, N8 // RING) as i:
                    for s in range(RING):
                        split_lo(L, i * RING + s, KT * P, s)
                for n in range(N8 // RING * RING, N8):
                    split_lo(L, n, KT * P, n % RING)
                split_lo(L, N8, HALF * P, N8 % RING)
                with pool.Fori(0, (N11 - 1) // RING) as i:
                    for s in range(RING):
                        n0 = N8 + 1 + s
                        split_lo(L, i * RING + n0, HALF * P, n0 % RING)

        @block.tensor
        def _(pe):
            def whalf(slot, part, k):
                at0 = (2 * slot + part) * HALF * P + k * P
                return W[:, at0:at0 + P]

            def three(out_, a, b, first, last, **kw):
                nc.tensor.matmul(out_, a[0], b[0], start=first, stop=False, **kw)
                nc.tensor.matmul(out_, a[0], b[1], start=False, stop=False, **kw)
                return nc.tensor.matmul(out_, a[1], b[0], start=False, stop=last, **kw)

            def wblock(L, n, slot, out_, rhs, ks, first, last):
                pe.wait_ge(w_ready.sem, w_ready.nth(L, n + 1))
                for i, k in enumerate(ks):
                    mm = three(out_, (whalf(slot, 0, i), whalf(slot, 1, i)),
                               (rhs[0][:, k * SEQ:(k + 1) * SEQ], rhs[1][:, k * SEQ:(k + 1) * SEQ]),
                               first and i == 0, last and i == len(ks) - 1)
                return mm

            Hs = [H[:, 0:KT * SEQ], H[:, KT * SEQ:2 * KT * SEQ]]

            def t_bank(L, use):
                u = T_USES.index(use)
                if u >= 2:
                    old = T_USES[u - 2]
                    pe.wait_ge(t_act.sem, t_act.after(L, old))
                    if old[0] in LO_OF:
                        pe.wait_ge(t_dve.sem, t_dve.after(L, (LO_OF[old[0]],) + old[1:]))
                return T[u % 2]

            def take_z(L, step):
                for b in banks_of(step):
                    if b in z_owner:
                        old = z_owner[b]
                        if old[0] == "z":
                            pe.wait_ge(w_exp.sem, w_exp.after(L, ("cum",) + old[1:]))
                        else:
                            pe.wait_ge(exps.sem, exps.after(L, old))
                    z_owner[b] = step

            z_owner = {}

            def rstd_sum(L, n):
                bank = t_bank(L, ("rstd", n))
                pe.wait_ge(prep, 3)
                pe.wait_ge(ssum_ready.sem, L * 2 + (n + 1))
                nc.tensor.matmul(bank[:, :], ones, ssum, start=True, stop=True).then_inc(t_ready.sem, 1)

            def step_proj(L, t, part):
                if part == 0:
                    if t >= 2:
                        pe.wait_ge(acc_free.sem, acc_free.after(L, ("ev", t - 2)))
                    pe.wait_ge(w_ready.sem, w_ready.nth(L, t + 1))
                for k in range(part * KT // PROJ_PARTS, (part + 1) * KT // PROJ_PARTS):
                    if t == 0:
                        pe.wait_ge(h_ready.sem, L * 16 + (k + 1))
                    mm = three(acc[t % 2][:, :], (whalf(t % RING, 0, k), whalf(t % RING, 1, k)),
                               (Hs[0][:, k * SEQ:(k + 1) * SEQ], Hs[1][:, k * SEQ:(k + 1) * SEQ]), k == 0, k == KT - 1)
                if part == PROJ_PARTS - 1:
                    mm.then_inc(blocks_done.sem, 1)

            def step_ms(L, t):
                bank = t_bank(L, ("ms", t))
                pe.wait_ge(sq_ready.sem, sq_ready.after(L, ("ev", t)))
                nc.tensor.matmul(bank[:, :], blk, SQ, start=True, stop=True).then_inc(t_ready.sem, 1)

            def step_vt(L, t):
                bank = t_bank(L, ("vt", t))
                pe.wait_ge(acc_free.sem, acc_free.after(L, ("ev", t)))
                for j in range(NB):
                    mm = nc.tensor.transpose(bank[:, j * P:(j + 1) * P], pbuf[:, (t % 2) * SEQ + j * P:(t % 2) * SEQ + (j + 1) * P], ident)
                mm.then_inc(t_ready.sem, 1)

            def tile_of(g, role):
                return TILES.index((g, role))

            def step_z(L, g, h):
                pe.wait_ge(qk_ready.sem, qk_ready.after(L, ("rl", tile_of(g, "k"))))
                take_z(L, ("z", g, h))
                r = slice(HD * h, HD * h + HD)
                q, k = qbuf[QSLOT[g, "q0"]], kbuf[g % 2]
                for j in range(NB):
                    keys, qs = slice(P * j, P * j + P), slice(P * j, SEQ)
                    nc.tensor.matmul(zpart(j), k[0][r, keys], q[0][r, qs], start=j < 3, stop=False, skip_group_check=True)
                    nc.tensor.matmul(zpart(j)[:, 0:P], identb, msb, start=False, stop=False, skip_group_check=True)
                    nc.tensor.matmul(zpart(j), k[0][r, keys], q[1][r, qs], start=False, stop=False, skip_group_check=True)
                    mm = nc.tensor.matmul(zpart(j), k[1][r, keys], q[0][r, qs], start=False, stop=True, skip_group_check=True)
                mm.then_inc(z_ready.sem, 1)

            def step_cum(L, g, h):
                pe.wait_ge(sp_ready.sem, sp_ready.after(L, ("sp", g, h)))
                for j in range(NB):
                    for i in range(NB - 1, j - 1, -1):
                        for part in range(2):
                            mm = nc.tensor.matmul(zpart(j, P * (i - j)), tri if i == j else neg1, epart(spb[part], i),
                                                  start=False, stop=(i == j and part == 1), skip_group_check=True)
                mm.then_inc(z_ready.sem, 1)

            def step_pv(L, g, h):
                kind = GROUPS[g][0]
                start = kind == "diff" or h % 2 == 0
                m = mix_tile(g, h // 2)
                if start and m:
                    pe.wait_ge(mix_ready.sem, mix_ready.after(L, m - 1))
                pe.wait_ge(t_dve.sem, t_dve.after(L, ("vl", tile_of(g, "v"))))
                if kind == "sb":
                    pe.wait_ge(w_split.sem, w_split.after(L, ("ws", g, h)))
                else:
                    pe.wait_ge(t_dve.sem, t_dve.after(L, ("xl", g, NB - 1 if kind == "diff" else (h, 1))))
                half = 0 if kind == "diff" else h % 2
                end = kind == "diff" or h % 2 == 1
                for j in range(NB):
                    qs = slice(P * j, min(P * (j + 2), SEQ) if kind == "swa" else SEQ)
                    vv = (vbuf[0][:, j, half, :], vbuf[1][:, j, half, :])
                    pp = (pt[0][:, j, qs], pt[1][:, j, qs])
                    mm = three(O[:, qs], vv, pp, start and j == 0, end and j == NB - 1, skip_group_check=True)
                mm.then_inc(pv_done.sem, 1)

            def step_s(L, g, b):
                kind = GROUPS[g][0]
                take_z(L, ("s", g, b))
                base = [512 * i for i in banks_of(("s", g, b))]
                if kind == "swa":
                    base.append(base[0] + 2 * P)
                kk = kbuf[g % 2]
                pe.wait_ge(qk_ready.sem, qk_ready.after(L, ("rl", tile_of(g, "k"))))
                parts = []
                for i in range(2):
                    if kind == "diff":
                        q, r = qbuf[QSLOT[g, "q0"]], slice(HD * i, HD * i + HD)
                        o = zall[:, base[i]:base[i] + P * (b + 1)]
                        parts.append((slice(P * b, P * b + P), slice(0, P * (b + 1)), o, o[:, P * b:P * b + P], mdf, True))
                    else:
                        hd, bp = b
                        q, r = qbuf[QSLOT[g, f"q{hd // 2}"]], slice(HD * (hd % 2), HD * (hd % 2) + HD)
                        bb = 2 * bp + i
                        lo = P if bb == 0 else 0
                        o = zall[:, base[i] + lo:base[i] + 2 * P]
                        parts.append((slice(P * bb, P * bb + P), slice(P * (bb - 1) + lo, P * (bb + 1)), o, o, mdf if bb == 0 else msw, i == 0))
                    qs, ks, o, m, mask, first = parts[-1]
                    nc.tensor.matmul(o, q[0][r, qs], kk[0][r, ks], start=first, stop=False, skip_group_check=True)
                    nc.tensor.matmul(m, identb, mask, start=False, stop=False, skip_group_check=True)
                    nc.tensor.matmul(o, q[0][r, qs], kk[1][r, ks], start=False, stop=False, skip_group_check=True)
                    mm = nc.tensor.matmul(o, q[1][r, qs], kk[0][r, ks], start=False, stop=True, skip_group_check=True)
                mm.then_inc(z_ready.sem, 1)

            def step_x(L, g, b):
                bank = t_bank(L, ("x", g, b))
                pe.wait_ge(at_ready.sem, at_ready.after(L, ("c", g, b)))
                src = at[steps("s").index(("s", g, b)) % 2]
                n0, n1 = (0, b + 1) if GROUPS[g][0] == "diff" else (1 if b[1] == 0 else 0, 4)
                for j in range(n0, n1):
                    mm = nc.tensor.transpose(bank[:, j * P:(j + 1) * P], src[:, j * P:(j + 1) * P], ident)
                mm.then_inc(t_ready.sem, 1)

            def step_mixn(L, g, i):
                bank = t_bank(L, ("mixn", g, i))
                pe.wait_ge(mix_act.sem, mix_act.after(L, ("mix", g, i)))
                nc.tensor.matmul(bank[:, :], ones, SQ, start=True, stop=True).then_inc(t_ready.sem, 1)

            def out_part(L, d, part):
                slot = (NT + d) % RING
                for k in WO_PARTS[part]:
                    mm = three(wobank[d % 3][:, :], (whalf(slot, 0, k), whalf(slot, 1, k)),
                               (mix[0][:, k * SEQ:(k + 1) * SEQ], mix[1][:, k * SEQ:(k + 1) * SEQ]), k == 0, k == KT - 1)
                return mm

            def step_wo(L, d, part):
                if part == 0:
                    pe.wait_ge(w_ready.sem, w_ready.nth(L, NT + d + 1))
                    if d < 2:
                        pe.wait_ge(acc_free.sem, acc_free.after(L, ("ev", NT - 2 + d)))
                    else:
                        pe.wait_ge(exps.sem, exps.after(L, [s for s in steps("s") if 0 in banks_of(s)][-1]))
                pe.wait_ge(mix_ready.sem, mix_ready.after(L, WO_PARTS[part][-1]))
                out_part(L, d, part)

            def out_tile(L, d):
                if d == 0:
                    pe.wait_ge(mix_ready.sem, mix_ready.after(L, KT - 1))
                if d >= 3:
                    pe.wait_ge(acc_free.sem, acc_free.nth(L, A_WO + d - 2))
                    pe.wait_ge(w_ready.sem, w_ready.nth(L, NT + d + 1))
                for part in range(3 if d < 3 else 0, 4):
                    mm = out_part(L, d, part)
                mm.then_inc(blocks_done.sem, 1)

            def gate_up(L, f, r, first=False):
                for i in range(2):
                    n = f * 2 + i
                    bank = gubank[2 * r + i]
                    if not first:
                        pe.wait_ge(acc_free.sem, acc_free.nth(L, n + (A_GU - 5)))
                    elif r == 0:
                        pe.wait_ge(acc_free.sem, acc_free.nth(L, A_GU - 1 + i))
                    if i == 0 and first and r == 0:
                        pe.wait_ge(h_ready.sem, L * 16 + 16)
                    mm = wblock(L, n + A_GU, (2 * r + i) % RING, bank[:, :], Hs, range(KT), True, True)
                    mm.then_inc(blocks_done.sem, 1)

            def down_tile(L, d, r):
                bank = downbank[r]
                pe.wait_ge(acc_free.sem, acc_free.nth(L, d + (A_DOWN - 2)))
                for half in range(2):
                    n = d * 2 + (N8 + half)
                    slot = (N8 + 2 * r + half) % RING
                    pe.wait_ge(w_ready.sem, w_ready.nth(L, n + 1))
                    for i in range(HALF):
                        k = HALF * half + i
                        if k in (0, FT - 1):
                            pe.wait_ge(ffr.sem, ffr.nth(L, FT - 1 if k == 0 else FT))
                        mm = three(bank[:, :], (whalf(slot, 0, i), whalf(slot, 1, i)),
                                   (ff[0][:, k * SEQ:(k + 1) * SEQ], ff[1][:, k * SEQ:(k + 1) * SEQ]), k == 0, k == FT - 1)
                    mm.then_inc(blocks_done.sem, 1)

            nc.tensor.sem_inc(blocks_done.sem, RING)
            with pe.Fori(0, DEPTH) as L:
                z_owner.clear()
                run = {"proj": step_proj, "rstd": rstd_sum, "ms": step_ms, "vt": step_vt, "z": step_z, "cum": step_cum,
                       "pv": step_pv, "s": step_s, "x": step_x, "mixn": step_mixn,
                       "wo": step_wo}
                for s in STEPS:
                    if s[0] in run:
                        run[s[0]](L, *s[1:])
                for d in range(KT):
                    out_tile(L, d)
                for r in range(3):
                    gate_up(L, r, r, first=True)
                    if r == 0:
                        rstd_sum(L, 1)
                with pe.Fori(1, FT // 3) as i:
                    for r in range(3):
                        gate_up(L, i * 3 + r, r)
                gate_up(L, FT - 1, 0)
                with pe.Fori(0, KT // 3) as i:
                    for r in range(3):
                        down_tile(L, i * 3 + r, r)
                for d in range(KT // 3 * 3, KT):
                    down_tile(L, d, d % 3)

        @block.scalar
        def _(act):
            A = nc.scalar.activation

            def load_functions(table_set):
                nc.scalar.add_instruction(mybir.InstLoadActFuncSet(
                    name=nc.get_next_instruction_name(), ins=[], outs=[], act_func_set_id=table_set))

            act.dma_start(misc[:, :], misc_in).then_inc(angles, 16)
            act.dma_start(pos.bitcast(I32), pos_in).then_inc(angles, 16)
            act.dma_start(gain0[:, :], par_in[:, 0:KT]).then_inc(gained, 16)
            for k in range(KT):
                act.dma_start(X[:, k * SEQ:(k + 1) * SEQ], x_in[k]).then_inc(xin[k], 16)
            act.dma_start(const[:, :], const_in[:, 0:3 * P]).then_inc(loaded, 16)
            act.dma_start(par[:, :], par_in[:, KT:]).then_inc(loaded, 16)
            act.dma_start(U[:, 0:NCONST - 3 * P], const_in[:, 3 * P:NCONST]).then_inc(loaded, 16)
            act.dma_start(lam, lam_in).then_inc(loaded, 16)

            def x_tile(d, gain, slot, waits):
                xs = X[:, bass.ds(d * SEQ, SEQ)]
                nc.scalar.drain()
                waits()
                A(H[:, bass.ds(d * SEQ, SEQ)], xs, ACT.Copy, scale=gain).then_inc(h_hi.sem, 1)
                A(sqbuf[slot], xs, ACT.Square).then_inc(x_sq.sem, 1)

            def w_split_hi(L, n, m, i=0):
                slot, cols = n % RING, (KT if n < N8 else HALF) * P
                act.wait_ge(blocks_done.sem, L * WPER + (i * m + (n + 1)))
                act.wait_ge(raw_ready[slot], L * (16 * WPER // RING) + (i * (16 * m // RING) + (n // RING + 1) * 16))
                A(W[:, 2 * slot * HALF * P:2 * slot * HALF * P + cols], raw[:, slot * HALF * P:slot * HALF * P + cols],
                  ACT.Copy).then_inc(w_hi.sem, 1)

            act.wait_ge(gained, 16)
            for k in range(KT):
                def waits(k=k):
                    act.wait_ge(xin[k], 16)
                    if k >= 3:
                        act.wait_ge(h_ready.sem, k - 1)
                x_tile(k, gain0[:, k:k + 1], k % 3, waits)
                if k == 2:
                    act.wait_ge(prep, 1)
                    A(tables[:, :], tables[:, :], ACT.Sin).then_inc(prep, 1)
            act.wait_ge(prep, 3)
            A(lamw[:, 2 * DEPTH:4 * DEPTH], lamw[:, 0:2 * DEPTH], ACT.Exp).then_inc(prep, 1)

            def norm(L, use, scale, dst, sig):
                act.wait_ge(t_ready.sem, t_ready.after(L, use))
                A(dst, T[T_USES.index(use) % 2][:, :], ACT.Ln, scale=scale, bias=eps).then_inc(t_act.sem, 1)
                nc.scalar.drain()
                A(dst, dst, ACT.Exp, scale=-0.5).then_inc(sig, 1)

            def slot_free(L, g):
                if g >= 2:
                    old = [s for s in steps("z", "cum", "s") if s[1] == g - 2][-1]
                    act.wait_ge(z_ready.sem, z_ready.after(L, old))

            def step_ev(L, t):
                g, role = TILES[t]
                src = pbuf[:, (t % 2) * SEQ:(t % 2 + 1) * SEQ]
                if roped(t):
                    act.wait_ge(acc_free.sem, acc_free.after(L, ("ev", t)))
                    old = before(("ev", t), "ms", "mixn")
                    if old is not None:
                        act.wait_ge(t_ready.sem, t_ready.after(L, old))
                    A(SQ, src, ACT.Square).then_inc(sq_ready.sem, 1)
                elif role != "v":
                    act.wait_ge(acc_free.sem, acc_free.after(L, ("ev", t)))
                    A(qk_buffer(g, role)[0], src, ACT.Copy).then_inc(qk_hi.sem, 1)
                w_split_hi(L, t + RING, 0)

            def step_ms(L, t):
                old = before(("ms", t), "ra")
                if old is not None:
                    act.wait_ge(rotated.sem, rotated.after(L, ("rb", old[1])))
                norm(L, ("ms", t), 1.0 / HD, RN, rn_ready.sem)

            def step_rb(L, t):
                g, role = TILES[t]
                slot_free(L, g)
                act.wait_ge(rotated.sem, rotated.after(L, ("rb", t)))
                A(qk_buffer(g, role)[0], Y, ACT.Copy).then_inc(qk_hi.sem, 1)

            def step_vt(L, t):
                g = TILES[t][0]
                use = ("vt", t)
                bank = T[T_USES.index(use) % 2][:, :].rearrange("p (j e) -> p j e", j=NB)
                act.wait_ge(t_ready.sem, t_ready.after(L, use))
                old = [s for s in steps("pv") if s[1] < g]
                if old:
                    assert before(use, "pv") == old[-1]
                    act.wait_ge(pv_done.sem, pv_done.after(L, old[-1]))
                else:
                    act.wait_ge(zeroed.sem, zeroed.after(L, 0))
                if GROUPS[g][0] == "diff":
                    A(vbuf[0][:, :, 0, :], bank, ACT.Copy).then_inc(t_act.sem, 1)
                else:
                    A(vbuf[0][:, :, 0, 0:HD], bank[:, :, 0:HD], ACT.Copy)
                    A(vbuf[0][:, :, 1, HD:P], bank[:, :, HD:P], ACT.Copy)
                    nc.scalar.drain().then_inc(t_act.sem, 1)

            def step_z(L, g, h):
                act.wait_ge(z_ready.sem, z_ready.after(L, ("z", g, h)))
                old = before(("z", g, h), "z")
                if old is not None:
                    act.wait_ge(w_split.sem, w_split.after(L, ("ws",) + old[1:]))
                for b, at0, n in ZE:
                    A(E[:, at0:at0 + n], Z[b][:, 0:n], ACT.Abs)
                nc.scalar.drain()
                A(E, E, ACT.Exp, scale=-1.0)
                nc.scalar.drain()
                A(E, E, ACT.Ln, bias=one).then_inc(ln_ready.sem, 1)

            def step_cum(L, g, h):
                act.wait_ge(z_ready.sem, z_ready.after(L, ("cum", g, h)))
                for b, at0, n in ZE:
                    A(E[:, at0:at0 + n], Z[b][:, 0:n], ACT.Exp)
                nc.scalar.drain().then_inc(w_exp.sem, 1)

            def step_s(L, g, b):
                k = steps("s").index(("s", g, b))
                st = (k % 4) * 8
                z0 = [512 * i for i in banks_of(("s", g, b))]
                act.wait_ge(negmax.sem, negmax.after(L, ("s", g, b)))
                if GROUPS[g][0] == "swa":
                    A(stat[:, st + 6:st + 8], stat[:, st + 2:st + 4], ACT.Exp, bias=cur[:, C_SINK + b[0]:C_SINK + b[0] + 1])
                for i in range(2):
                    lo, hi, e = exp_columns(g, b, i)
                    z = z0[i] if GROUPS[g][0] == "diff" else z0[0]
                    A(e[:, lo:hi], zall[:, z + lo:z + hi], ACT.Exp, bias=stat[:, st + 2 + i:st + 3 + i],
                      accum_out=stat[:, st + 4 + i:st + 5 + i])
                nc.scalar.drain().then_inc(exps.sem, 1)

            def step_x(L, g, b):
                use = ("x", g, b)
                act.wait_ge(t_ready.sem, t_ready.after(L, use))
                act.wait_ge(pv_done.sem, pv_done.after(L, before(use, "pv")))
                bank = T[T_USES.index(use) % 2][:, :].rearrange("p (j e) -> p j e", j=NB)
                for js, q, c0, c1 in pt_parts(use):
                    last = A(pt[0][:, js, q * P:(q + 1) * P], bank[:, c0:c1, :], ACT.Copy)
                if GROUPS[g][0] == "diff":
                    last.then_inc(t_act.sem, 1)
                else:
                    nc.scalar.drain().then_inc(t_act.sem, 1)

            def step_mix(L, g, i):
                m = mix_tile(g, i)
                act.wait_ge(pv_done.sem, pv_done.after(L, ("pv", g, 0 if GROUPS[g][0] == "diff" else 2 * i + 1)))
                if GROUPS[g][0] == "diff":
                    act.wait_ge(t_ready.sem, t_ready.after(L, before(("mix", g, i), "ms", "mixn")))
                    A(SQ, O[:, :], ACT.Square).then_inc(mix_act.sem, 1)
                else:
                    A(mix[0][:, m * SEQ:(m + 1) * SEQ], O[:, :], ACT.Copy).then_inc(mix_act.sem, 1)

            def step_mixn(L, g, i):
                norm(L, ("mixn", g, i), 1.0 / P, MRN[:, :], mrn_ready.sem)

            def silu_tile(L, f, r):
                nc.scalar.drain()
                act.wait_ge(acc_free.sem, acc_free.nth(L, f * 2 + (A_GU + 1)))
                act.wait_ge(loaded, 16)
                A(gbuf[r], gbuf[r], ACT.Silu).then_inc(silu.sem, 1)

            def gate_up(L, f, r, i=0):
                w_split_hi(L, A_GU + 2 * f + RING, 6, i)
                silu_tile(L, i * 3 + f, r)
                w_split_hi(L, A_GU + 2 * f + 1 + RING, 6, i)

            def down(L, d, i=0):
                for half in range(2):
                    if N8 + 2 * d + half + RING < WPER:
                        w_split_hi(L, N8 + 2 * d + half + RING, 6, i)

                def waits():
                    act.wait_ge(acc_free.sem, acc_free.nth(L, i * 3 + (d + A_DOWN + 1)))
                    act.wait_ge(loaded, 16)
                x_tile(i * 3 + d, cur[:, bass.ds(i * 3 + (d + C_NG), 1)], d % 3, waits)

            with act.Fori(0, DEPTH) as L:
                load_functions(6)
                norm(L, ("rstd", 0), 1.0 / D_MODEL, rstd[:, :], rstd_ready.sem)
                run = {"ev": step_ev, "ms": step_ms, "rb": step_rb, "vt": step_vt, "z": step_z, "cum": step_cum,
                       "s": step_s, "x": step_x, "mix": step_mix, "mixn": step_mixn}
                for s in STEPS:
                    if s[0] in run:
                        nc.scalar.drain()
                        run[s[0]](L, *s[1:])
                for d in range(KT):
                    w_split_hi(L, A_WO + d + RING, 0)

                    def waits(d=d):
                        act.wait_ge(acc_free.sem, acc_free.nth(L, A_WO + d + 1))
                    x_tile(d, cur[:, C_FG + d:C_FG + d + 1], d % 3, waits)
                for n in range(2):
                    w_split_hi(L, A_GU + n + RING, 0)
                norm(L, ("rstd", 1), 1.0 / D_MODEL, rstd[:, :], rstd_ready.sem)
                load_functions(18)
                silu_tile(L, 0, 0)
                with act.Fori(0, FT // 3 - 1) as i:
                    load_functions(18)
                    for f in range(1, 4):
                        gate_up(L, f, f % 3, i)
                for f in range(FT // 3 * 3 - 2, FT):
                    gate_up(L, f, f % 3)
                with act.Fori(0, KT // 3) as i:
                    for d in range(3):
                        down(L, d, i)
                for d in range(KT // 3 * 3, KT):
                    down(L, d)

        @block.vector
        def _(dve):
            V = nc.vector
            drain = V.drain
            tt, ts, stt, cp = V.tensor_tensor, V.tensor_scalar, V.scalar_tensor_tensor, V.tensor_copy

            def x_tile(d, gain):
                xs = X[:, bass.ds(d * SEQ, SEQ)]
                stt(H[:, bass.ds(d * SEQ + KT * SEQ, SEQ)], xs, gain, H[:, bass.ds(d * SEQ, SEQ)].bitcast(F32),
                    ALU.mult, ALU.subtract).then_inc(h_ready.sem, 1)

            def square_sum(slot):
                return tt(ssum, ssum, sqbuf[slot], ALU.add)

            TWO_PI = 2 * np.pi
            C1 = 6.28125
            C2 = float(np.float32(TWO_PI - C1))
            C3 = float(np.float32(TWO_PI - C1 - C2))
            MAGIC = 1.5 * 2.0 ** 23
            PI = 3.1415925
            dve.wait_ge(angles, 2 * 16)
            cp(work[:, 0:SEQ], pos.bitcast(I32))
            drain()
            ts(work[:, 0:SEQ], work[:, 0:SEQ], misc[:, 0:1], None, ALU.mult)
            drain()
            for i, turn in ((0, 0.25), (1, 0.0)):
                n, r = work[:, (1 + i) * SEQ:(2 + i) * SEQ], tables[:, i * SEQ:(i + 1) * SEQ]
                ts(n, work[:, 0:SEQ], 1.0 / TWO_PI, turn, ALU.mult, ALU.add)
                drain()
                ts(n, n, MAGIC, MAGIC, ALU.add, ALU.subtract)
                drain()
                stt(r, n, -C1, work[:, 0:SEQ], ALU.mult, ALU.add)
                drain()
                stt(r, n, -C2, r, ALU.mult, ALU.add)
                drain()
                stt(r, n, -C3, r, ALU.mult, ALU.add)
                drain()
                if i == 0:
                    ts(r, r, np.pi / 2, None, ALU.add)
                    drain()
                ts(r, r, PI, -PI, ALU.min, ALU.max)
            drain().then_inc(prep, 1)
            V.memset(ssum, 0.0)
            dve.wait_ge(gained, 16)
            for k in range(KT):
                drain()
                dve.wait_ge(h_hi.sem, k + 1)
                x_tile(k, gain0[:, k:k + 1])
                dve.wait_ge(x_sq.sem, k + 1)
                square_sum(k % 3)
            drain().then_inc(ssum_ready.sem, 1)

            dve.wait_ge(loaded, 4 * 16)
            cp(constr[:, :], U[:, 0:2 * P])
            cp(constb[:, P:4 * P], U[:, 2 * P:5 * P])
            cp(constb[:, 0:P], ident)
            dve.wait_ge(prep, 2)
            ts(SIN, SIN, misc[:, 1:2], None, ALU.mult)
            for l in range(DEPTH):
                for i in range(2):
                    a = lam[:, (4 * l + 2 * i) * HD:(4 * l + 2 * i + 1) * HD]
                    tt(a, a, lam[:, (4 * l + 2 * i + 1) * HD:(4 * l + 2 * i + 2) * HD], ALU.mult)
                    drain()
                    V.reduce_sum(lamw[:, 2 * l + i:2 * l + i + 1], a, AX_X)
            drain().then_inc(prep, 1)
            dve.wait_ge(prep, 4)
            for l in range(DEPTH):
                o = 2 * DEPTH + 2 * l
                nl = par[:, l * NPAR + C_NLAM:l * NPAR + C_NLAM + 1]
                tt(nl, lamw[:, o + 1:o + 2], lamw[:, o:o + 1], ALU.subtract)
                drain()
                tt(nl, nl, misc[:, 4 + l:5 + l], ALU.subtract)
                g = par[:, l * NPAR + C_SUB:l * NPAR + C_SUB + 1]
                tt(g, g, misc[:, 6 + l:7 + l], ALU.mult)
                for c in (C_DQ, C_WQ):
                    g = par[:, l * NPAR + c:l * NPAR + c + 1]
                    ts(g, g, SCALE, None, ALU.mult)
            drain()

            def step_ev(L, t):
                g, role = TILES[t]
                if t == 0:
                    dve.wait_ge(rstd_ready.sem, rstd_ready.after(L, ("rstd", 0)))
                dve.wait_ge(blocks_done.sem, blocks_done.nth(L, t + 1))
                c = SCALE if role == "q0" and GROUPS[g][0] == "sb" else 1.0
                stt(pbuf[:, (t % 2) * SEQ:(t % 2 + 1) * SEQ], acc[t % 2][:, :], c, rstd[:, :], ALU.mult, ALU.mult)\
                    .then_inc(acc_free.sem, 1)
                if t == 1:
                    V.memset(vbuf[0].bitcast(F32), 0.0)
                    V.memset(vbuf[1].bitcast(F32), 0.0)
                    drain().then_inc(zeroed.sem, 1)

            def step_ra(L, t):
                g, role = TILES[t]
                gain = {"diff": {"q0": C_DQ, "k": C_DK}, "swa": {"q0": C_WQ, "q1": C_WQ, "k": C_WK}}[GROUPS[g][0]][role]
                old = before(("ra", t), "rl")
                if old is not None and roped(old[1]):
                    dve.wait_ge(qk_hi.sem, qk_hi.after(L, old))
                dve.wait_ge(rn_ready.sem, rn_ready.after(L, ("ms", t)))
                stt(Y, pbuf[:, (t % 2) * SEQ:(t % 2 + 1) * SEQ], cur[:, gain:gain + 1], RN, ALU.mult, ALU.mult)
                drain()
                V.stream_shuffle(ROT, Y, [(i + 16) % 32 for i in range(32)])
                tt(Y, Y, COS, ALU.mult)

            def step_rb(L, t):
                tt(ROT, ROT, SIN, ALU.mult)
                drain()
                tt(Y, Y, ROT, ALU.add).then_inc(rotated.sem, 1)

            def step_rl(L, t):
                g, role = TILES[t]
                hi, lo = qk_buffer(g, role)
                src = Y if roped(t) else pbuf[:, (t % 2) * SEQ:(t % 2 + 1) * SEQ]
                dve.wait_ge(qk_hi.sem, qk_hi.after(L, ("rl", t)))
                tt(lo, src, hi.bitcast(F32), ALU.subtract).then_inc(qk_ready.sem, 1)

            def step_vl(L, t):
                bank = T[T_USES.index(("vt", t)) % 2][:, :].rearrange("p (j e) -> p j e", j=NB)
                dve.wait_ge(t_act.sem, t_act.after(L, ("vt", t)))
                hi, lo = vbuf
                if GROUPS[TILES[t][0]][0] == "diff":
                    tt(lo[:, :, 0, :], bank, hi[:, :, 0, :].bitcast(F32), ALU.subtract).then_inc(t_dve.sem, 1)
                else:
                    tt(lo[:, :, 0, 0:HD], bank[:, :, 0:HD], hi[:, :, 0, 0:HD].bitcast(F32), ALU.subtract)
                    tt(lo[:, :, 1, HD:P], bank[:, :, HD:P], hi[:, :, 1, HD:P].bitcast(F32), ALU.subtract)
                    drain().then_inc(t_dve.sem, 1)

            def step_sp(L, g, h):
                dve.wait_ge(ln_ready.sem, ln_ready.after(L, ("z", g, h)))
                for b, at0, n in ZE:
                    stt(E[:, at0:at0 + n], Z[b][:, 0:n], 0.0, E[:, at0:at0 + n], ALU.max, ALU.add)
                drain()
                cp(spb[0], E)
                drain()
                tt(spb[1], E, spb[0].bitcast(F32), ALU.subtract).then_inc(sp_ready.sem, 1)

            def step_ws(L, g, h):
                dve.wait_ge(w_exp.sem, w_exp.after(L, ("cum", g, h)))
                old = before(("ws", g, h), "pv")
                if old is not None:
                    dve.wait_ge(pv_done.sem, pv_done.after(L, old))
                for j in range(NB):
                    cp(pt[0][:, j, P * j:SEQ], epart(E, j))
                drain()
                for j in range(NB):
                    tt(pt[1][:, j, P * j:SEQ], epart(E, j), pt[0][:, j, P * j:SEQ].bitcast(F32), ALU.subtract)
                drain().then_inc(w_split.sem, 1)

            def step_s(L, g, b):
                st = (steps("s").index(("s", g, b)) % 4) * 8
                used = banks_of(("s", g, b))
                at0 = 512 * used[0]
                dve.wait_ge(z_ready.sem, z_ready.after(L, ("s", g, b)))
                if GROUPS[g][0] == "diff":
                    z = zall[:, :].rearrange("p (c k) -> p c k", c=3)[:, used[0]:used[1] + 1:used[1] - used[0], 0:P * (b + 1)]
                    V.reduce_max(stat[:, st:st + 2], z, AX_X)
                    drain()
                    ts(stat[:, st + 2:st + 4], stat[:, st:st + 2], -1.0, None, ALU.mult).then_inc(negmax.sem, 1)
                else:
                    hd, bp = b
                    if bp == 0:
                        V.reduce_max(stat[:, st:st + 1], zall[:, at0 + P:at0 + 2 * P], AX_X)
                        V.reduce_max(stat[:, st + 1:st + 2], zall[:, at0 + 2 * P:at0 + 4 * P], AX_X)
                    else:
                        V.reduce_max(stat[:, st:st + 2], zall[:, at0:at0 + 4 * P].rearrange("p (b k) -> p b k", b=2), AX_X)
                    drain()
                    ts(stat[:, st + 2:st + 4], stat[:, st:st + 2], cur[:, C_SINK + hd:C_SINK + hd + 1], -1.0,
                       ALU.max, ALU.mult).then_inc(negmax.sem, 1)

            def step_c(L, g, b):
                k = steps("s").index(("s", g, b))
                st = (k % 4) * 8
                dve.wait_ge(exps.sem, exps.after(L, ("s", g, b)))
                if k >= 2:
                    old = steps("s")[k - 2]
                    dve.wait_ge(t_ready.sem, t_ready.after(L, ("x",) + old[1:]))
                dst = at[k % 2]
                (lo0, hi0, e0), (lo1, hi1, e1) = exp_columns(g, b, 0), exp_columns(g, b, 1)
                if GROUPS[g][0] == "diff":
                    V.reciprocal(stat[:, st + 6:st + 8], stat[:, st + 4:st + 6])
                    drain()
                    ts(e1[:, 0:hi1], e1[:, 0:hi1], stat[:, st + 7:st + 8], cur[:, C_NLAM:C_NLAM + 1], ALU.mult, ALU.mult)
                    drain()
                    stt(dst[:, 0:hi0], e0[:, 0:hi0], stat[:, st + 6:st + 7], e1[:, 0:hi0], ALU.mult, ALU.add).then_inc(at_ready.sem, 1)
                else:
                    tt(stat[:, st + 4:st + 6], stat[:, st + 4:st + 6], stat[:, st + 6:st + 8], ALU.add)
                    drain()
                    V.reciprocal(stat[:, st + 6:st + 8], stat[:, st + 4:st + 6])
                    drain()
                    ts(dst[:, lo0:hi0], e0[:, lo0:hi0], stat[:, st + 6:st + 7], None, ALU.mult)
                    ts(dst[:, lo1:hi1], e1[:, lo1:hi1], stat[:, st + 7:st + 8], None, ALU.mult)
                    drain().then_inc(at_ready.sem, 1)

            def step_xl(L, g, b):
                use = ("x", g, b)
                dve.wait_ge(t_act.sem, t_act.after(L, use))
                bank = T[T_USES.index(use) % 2][:, :].rearrange("p (j e) -> p j e", j=NB)
                for js, q, c0, c1 in pt_parts(use):
                    last = tt(pt[1][:, js, q * P:(q + 1) * P], bank[:, c0:c1, :], pt[0][:, js, q * P:(q + 1) * P].bitcast(F32), ALU.subtract)
                if GROUPS[g][0] == "diff":
                    last.then_inc(t_dve.sem, 1)
                else:
                    drain().then_inc(t_dve.sem, 1)

            def step_mixl(L, g, i):
                m = mix_tile(g, i)
                hi, lo = (mix[part][:, m * SEQ:(m + 1) * SEQ] for part in range(2))
                if GROUPS[g][0] == "diff":
                    dve.wait_ge(mrn_ready.sem, mrn_ready.after(L, ("mixn", g, i)))
                    stt(MRN[:, :], O[:, :], cur[:, C_SUB:C_SUB + 1], MRN[:, :], ALU.mult, ALU.mult)
                    drain()
                    cp(hi, MRN[:, :])
                    drain()
                    tt(lo, MRN[:, :], hi.bitcast(F32), ALU.subtract).then_inc(mix_ready.sem, 1)
                else:
                    dve.wait_ge(mix_act.sem, mix_act.after(L, ("mix", g, i)))
                    tt(lo, O[:, :], hi.bitcast(F32), ALU.subtract).then_inc(mix_ready.sem, 1)

            def gate_up(L, f, r):
                g, u = gubank[2 * r], gubank[2 * r + 1]
                drain()
                dve.wait_ge(rstd_ready.sem, rstd_ready.after(L, ("rstd", 1)))
                dve.wait_ge(blocks_done.sem, blocks_done.nth(L, f * 2 + (A_GU + 1)))
                tt(gbuf[r], g[:, :], rstd[:, :], ALU.mult).then_inc(acc_free.sem, 1)
                dve.wait_ge(blocks_done.sem, blocks_done.nth(L, f * 2 + (A_GU + 2)))
                tt(ubuf[r], u[:, :], rstd[:, :], ALU.mult).then_inc(acc_free.sem, 1)
                drain()
                dve.wait_ge(silu.sem, silu.nth(L, f + 1))
                tt(ubuf[r], ubuf[r], gbuf[r], ALU.mult)
                drain()
                cp(ff[0][:, bass.ds(f * SEQ, SEQ)], ubuf[r])
                drain()
                tt(ff[1][:, bass.ds(f * SEQ, SEQ)], ubuf[r], ff[0][:, bass.ds(f * SEQ, SEQ)].bitcast(F32), ALU.subtract)\
                    .then_inc(ffr.sem, 1)

            def x_stage_tile(L, blocks, n0, d, bank, gain):
                xs = X[:, bass.ds(d * SEQ, SEQ)]
                drain()
                dve.wait_ge(blocks_done.sem, blocks_done.nth(L, blocks))
                tt(xs, xs, bank[:, :], ALU.add).then_inc(acc_free.sem, 1)
                drain()
                dve.wait_ge(h_hi.sem, h_hi.nth(L, d + (n0 + 1)))
                x_tile(d, gain)
                dve.wait_ge(x_sq.sem, x_sq.nth(L, d + (n0 + 1)))
                square_sum(d % 3)

            with dve.Fori(0, DEPTH) as L:
                cp(cur[:, :], par[:, bass.ds(L * NPAR, NPAR)])
                drain()
                run = {"ev": step_ev, "ra": step_ra, "rb": step_rb, "rl": step_rl, "vl": step_vl, "sp": step_sp,
                       "ws": step_ws, "s": step_s, "c": step_c, "xl": step_xl, "mixl": step_mixl}
                for s in STEPS:
                    if s[0] in run:
                        drain()
                        run[s[0]](L, *s[1:])
                V.memset(ssum, 0.0)
                drain()
                for d in range(KT):
                    x_stage_tile(L, NT + d + 1, 0, d, wobank[d % 3], cur[:, C_FG + d:C_FG + d + 1])
                drain().then_inc(ssum_ready.sem, 1)
                with dve.Fori(0, FT // 3) as i:
                    for r in range(3):
                        gate_up(L, i * 3 + r, r)
                gate_up(L, FT - 1, 0)
                V.memset(ssum, 0.0)
                drain()
                for d in range(KT):
                    x_stage_tile(L, N8 + 2 * d + 2, KT, d, downbank[d % 3], cur[:, C_NG + d:C_NG + d + 1])
                drain().then_inc(ssum_ready.sem, 1)


def _launch_layout(inputs):
    f32 = np.float32
    g = {k: np.asarray(v) for k, v in inputs.items()}
    perm = np.concatenate([np.arange(0, 16), np.arange(32, 48), np.arange(16, 32), np.arange(48, 64)])
    perm2 = np.concatenate([perm, HD + perm])
    sbw, dqk, dw = 256, 512, 512
    o_sq, o_sk, o_sv = 0, sbw, 2 * sbw
    o_dq, o_dk, o_dv = 3 * sbw, 3 * sbw + dqk, 3 * sbw + 2 * dqk
    o_wq = o_dv + dw
    o_wk, o_wv = o_wq + 256, o_wq + 256 + 128
    cols = []
    for (grp, role) in TILES:
        kind, i = GROUPS[grp]
        if kind == "sb":
            cols.append({"q0": o_sq, "k": o_sk, "v": o_sv}[role] + i * P + np.arange(P))
        elif kind == "diff":
            cols.append({"q0": o_dq, "k": o_dk, "v": o_dv}[role] + i * P + (np.arange(P) if role == "v" else perm2))
        elif role[0] == "q":
            t = int(role[1])
            cols.append(o_wq + np.concatenate([t * HD + perm, (t + 2) * HD + perm]))
        else:
            cols.append({"k": o_wk + perm2, "v": o_wv + np.arange(P)}[role])
    cols = np.concatenate(cols)
    c0 = sbw + dw
    rows = np.concatenate([np.arange(sbw)] + [c0 + h * HD + np.arange(HD) for h in (0, 2, 1, 3)] + [sbw + np.arange(dw)])

    def blocks(w):
        return w.reshape(w.shape[0] // P, P, w.shape[1] // P, P).transpose(2, 1, 0, 3)
    w8, w11 = [], []
    for l in range(DEPTH):
        w8.append(blocks(g["w_in"][l][:, cols]))
        w8.append(blocks(g["w_o"][l][rows]))
        gu = np.stack([blocks(g["w_gate"][l]), blocks(g["w_up"][l])], axis=1)
        w8.append(gu.reshape(2 * FT, P, KT, P))
        w11.append(blocks(g["w_down"][l]).reshape(KT, P, 2, HALF, P).transpose(0, 2, 1, 3, 4).reshape(N11, P, HALF, P))
    w8 = np.concatenate(w8).reshape(DEPTH * N8, P, KT * P)
    w11 = np.concatenate(w11).reshape(DEPTH * N11, P, HALF * P)
    par = [g["attn_norm_g"][0].reshape(KT, P).T]
    for l in range(DEPTH):
        two = lambda v: np.concatenate([v[l][perm], v[l][perm]])[:, None]
        nxt = g["attn_norm_g"][(l + 1) % DEPTH]
        par += [g["ffn_norm_g"][l].reshape(KT, P).T, nxt.reshape(KT, P).T,
                two(g["diff_q_norm_g"]), two(g["diff_k_norm_g"]), two(g["swa_q_norm_g"]), two(g["swa_k_norm_g"]),
                g["diff_subln_g"][l][:, None],
                np.tile(g["swa_sinks"][l][[0, 2, 1, 3]][None, :], (P, 1)), np.zeros((P, 1), f32)]
    par = np.concatenate(par, axis=1)
    lam = np.tile(g["diff_lambda"].reshape(1, -1), (P, 1))
    misc = np.zeros((P, 8), f32)
    inv = f32(1) / f32(ROPE_THETA) ** (np.arange(0, HD, 2, dtype=f32) / f32(HD))
    misc[:, 0] = inv[perm2 % HD % 32]
    misc[:, 1] = np.where(perm2 % HD < 32, -1.0, 1.0)
    misc[:, 2] = EPS
    misc[:, 3] = 1.0
    for l in range(DEPTH):
        li = 0.8 - 0.6 * np.exp(-0.3 * l)
        misc[:, 4 + l], misc[:, 6 + l] = li, 1.0 - li
    i, j = np.arange(P)[:, None], np.arange(P)[None, :]
    const = np.zeros((P, NCONST), f32)
    const[:, K_ID:K_ID + P] = i == j
    const[:, K_BLK:K_BLK + P] = i // HD == j // HD
    const[:, K_ONE:K_ONE + P] = 1.0
    const[:, K_TRI:K_TRI + P] = -1.0 * (i >= j)
    const[:, K_NEG1:K_NEG1 + P] = -1.0
    const[:, K_MSB:K_MSB + P] = NEG * (i >= j)
    const[:, K_MSW:K_MSW + P] = NEG * ((j < CHUNK) | (i >= CHUNK))
    const[:, K_MDF:K_MDF + P] = NEG * ((i < CHUNK) & (j >= CHUNK))
    x = g["x"].reshape(SEQ, KT, P).transpose(1, 2, 0)
    pos = np.tile(g["positions"].reshape(1, SEQ), (P, 1))
    return [("x", x), ("pos", pos), ("w8", w8), ("w11", w11), ("par", par), ("lam", lam), ("misc", misc), ("const", const)]


def kernel(**inputs):
    import concourse.bacc as _bacc
    from concourse.bass_utils import run_bass_kernel_spmd as _run

    nc = _bacc.Bacc("TRN2", target_bir_lowering=False, num_devices=1, dynamic_dma_scratch_size=1024)
    arrays, args = {}, []
    for name, a in _launch_layout(inputs):
        a = np.ascontiguousarray(a)
        arrays[f"in_{name}"] = a
        args.append(nc.dram_tensor(f"in_{name}", a.shape, mybir.dt.from_np(a.dtype), kind="ExternalInput").ap())
    out = nc.dram_tensor("out_x", (KT, P, SEQ), F32, kind="ExternalOutput").ap()
    trunk_kernel(nc, *args, out)
    r = _run(nc, [arrays], core_ids=[0])
    y = r.results[0]["out_x"]
    return np.ascontiguousarray(y.transpose(2, 0, 1).reshape(1, SEQ, D_MODEL))
```
